# Optimizing a Trainium2 kernel written in Bass

```python
import math
import jax, jax.numpy as jnp
from jax import lax
import numpy as np

D_MODEL = 1024
BATCH = 1
SEQ = 512
DEPTH = 2

GLA_HEADS = 4
GLA_DK = 64
GLA_DV = 128
GLA_RANK = 16
GLA_TAU = 16.0
GLA_CHUNK = 64
DIFF_HEADS = 4
DIFF_DH = 64
DIFF_DV = 2 * DIFF_DH
Q_BLOCK = 128
A_QK = GLA_HEADS * GLA_DK
A_V = GLA_HEADS * GLA_DV
B_QK = DIFF_HEADS * 2 * DIFF_DH
B_V = DIFF_HEADS * DIFF_DV
EVEN_IN = 2 * A_QK + 2 * A_V + GLA_RANK + 2 * B_QK + B_V
EVEN_MIX = A_V + B_V
DIL_PATTERNS = ((128, 1), (512, 4), (2048, 16))
DIL_GROUPS = 3
DIL_HEADS = 4
DIL_DH = 128
ODD_IN = DIL_GROUPS * 3 * DIL_HEADS * DIL_DH
ODD_MIX = DIL_HEADS * DIL_DH
D_FF = 2816
CONV_W = 3
EPS = 1e-6
N_EVEN = (DEPTH + 1) // 2
N_ODD = DEPTH // 2


def rmsnorm(x, g):
    xf = x.astype(jnp.float32)
    y = xf * lax.rsqrt(jnp.mean(xf * xf, axis=-1, keepdims=True) + EPS)
    return (y * g.astype(jnp.float32)).astype(x.dtype)

def gla(q, k, v, log_a):
    B, S, H, dk = q.shape
    dv = v.shape[-1]
    C = GLA_CHUNK
    N = S // C
    f32 = jnp.float32

    def chunk(t):
        return t.astype(f32).reshape(B, N, C, H, t.shape[-1]).transpose(0, 3, 1, 2, 4)

    qc, kc, vc, lc = chunk(q * (dk ** -0.5)), chunk(k), chunk(v), chunk(log_a)
    b = jnp.cumsum(lc, axis=3)
    b_last = b[:, :, :, -1:, :]
    q_d = qc * jnp.exp(b)
    k_d = kc * jnp.exp(-b)
    causal = jnp.tril(jnp.ones((C, C), dtype=bool))
    att = jnp.where(causal, jnp.einsum('bhnik,bhnjk->bhnij', q_d, k_d), 0.0)
    o_intra = jnp.einsum('bhnij,bhnjv->bhniv', att, vc)
    kv = jnp.einsum('bhnjk,bhnjv->bhnkv', kc * jnp.exp(b_last - b), vc)
    decay = jnp.exp(b_last[:, :, :, 0, :])

    def step(state, inp):
        kv_n, dec_n = inp
        return dec_n[..., None] * state + kv_n, state

    s0 = jnp.zeros((B, H, dk, dv), f32)
    _, states = lax.scan(step, s0, (jnp.moveaxis(kv, 2, 0), jnp.moveaxis(decay, 2, 0)))
    states = jnp.moveaxis(states, 0, 2)
    o = o_intra + jnp.einsum('bhnik,bhnkv->bhniv', q_d, states)
    return o.transpose(0, 2, 3, 1, 4).reshape(B, S, H, dv).astype(v.dtype)

def diff_attention(q, k, v, lam):
    B, S, H, _, dh = q.shape
    dv = v.shape[-1]
    nb = S // Q_BLOCK
    qb = (q * (dh ** -0.5)).reshape(B, nb, Q_BLOCK, H, 2, dh).transpose(1, 0, 3, 4, 2, 5)
    kt = k.transpose(0, 2, 3, 1, 4)
    vt = v.transpose(0, 2, 1, 3)
    kpos = jnp.arange(S)

    def block(args):
        qblk, n = args
        s = jnp.einsum('bhcqd,bhckd->bhcqk', qblk, kt).astype(jnp.float32)
        qpos = n * Q_BLOCK + jnp.arange(Q_BLOCK)
        s = jnp.where(kpos[None, :] <= qpos[:, None], s, -jnp.inf)
        p = jax.nn.softmax(s, axis=-1)
        w = p[:, :, 0] - lam * p[:, :, 1]
        return jnp.einsum('bhqk,bhkv->bhqv', w.astype(vt.dtype), vt)

    o = lax.map(block, (qb, jnp.arange(nb)))
    return o.transpose(1, 0, 3, 2, 4).reshape(B, S, H, dv)

def dilated_branch(q, k, v, dilation, wc):
    B, S, H, dh = q.shape
    L = S // dilation
    nb = -(-L // wc)
    Lp = nb * wc

    def to_class(t):
        t = t.reshape(B, L, dilation, H, dh).transpose(0, 2, 3, 1, 4)
        t = jnp.pad(t, ((0, 0), (0, 0), (0, 0), (0, Lp - L), (0, 0)))
        return t.reshape(B, dilation, H, nb, wc, dh)

    def band(t):
        prev = jnp.pad(t, ((0, 0),) * 3 + ((1, 0), (0, 0), (0, 0)))[:, :, :, :-1]
        return jnp.concatenate([prev, t], axis=-2)

    qc = to_class(q)
    kb = band(to_class(k))
    vb = band(to_class(v))
    s = jnp.einsum('brhnqd,brhnkd->brhnqk', qc, kb).astype(jnp.float32) * (dh ** -0.5)
    i = jnp.arange(wc)[:, None]
    j = jnp.arange(2 * wc)[None, :]
    dist = i + wc - j
    blk = jnp.arange(nb)[:, None, None]
    valid = (dist >= 0) & (dist <= wc) & ((blk > 0) | (j >= wc))
    s = jnp.where(valid, s, -jnp.inf)
    lse = jax.nn.logsumexp(s, axis=-1)
    p = jnp.exp(s - lse[..., None])
    o = jnp.einsum('brhnqk,brhnkd->brhnqd', p.astype(vb.dtype), vb)
    o = o.reshape(B, dilation, H, Lp, dh)[:, :, :, :L].transpose(0, 3, 1, 2, 4).reshape(B, S, H, dh)
    lse = lse.reshape(B, dilation, H, Lp)[..., :L].transpose(0, 3, 1, 2).reshape(B, S, H)
    return o, lse

def even_mixer(h, w_in, w_a2, b_a, gla_gain, dq_gain, dk_gain, lq1, lk1, lq2, lk2, diff_gain, w_out, lambda_init):
    B, S, _ = h.shape
    z = h @ w_in
    sizes = [A_QK, A_QK, A_V, A_V, GLA_RANK, B_QK, B_QK]
    aq, ak, av, ag, ar, bq, bk, bv = jnp.split(z, [int(c) for c in np.cumsum(sizes)], axis=-1)
    log_a = jax.nn.log_sigmoid((ar @ w_a2 + b_a).astype(jnp.float32)) / GLA_TAU
    oa = gla(aq.reshape(B, S, GLA_HEADS, GLA_DK), ak.reshape(B, S, GLA_HEADS, GLA_DK),
             av.reshape(B, S, GLA_HEADS, GLA_DV), log_a.reshape(B, S, GLA_HEADS, GLA_DK))
    oa = rmsnorm(oa, gla_gain) * jax.nn.silu(ag.reshape(B, S, GLA_HEADS, GLA_DV))
    bq = rmsnorm(bq.reshape(B, S, DIFF_HEADS, 2, DIFF_DH), dq_gain)
    bk = rmsnorm(bk.reshape(B, S, DIFF_HEADS, 2, DIFF_DH), dk_gain)
    f32 = jnp.float32
    lam = (jnp.exp(jnp.sum(lq1.astype(f32) * lk1.astype(f32)))
           - jnp.exp(jnp.sum(lq2.astype(f32) * lk2.astype(f32))) + lambda_init)
    ob = diff_attention(bq, bk, bv.reshape(B, S, DIFF_HEADS, DIFF_DV), lam)
    ob = rmsnorm(ob, diff_gain) * (1.0 - lambda_init)
    o = jnp.concatenate([oa.reshape(B, S, A_V), ob.reshape(B, S, B_V)], axis=-1)
    return o @ w_out

def odd_mixer(h, w_in, q_gain, k_gain, w_out):
    B, S, _ = h.shape
    z = (h @ w_in).reshape(B, S, DIL_GROUPS, 3, DIL_HEADS, DIL_DH)
    q = rmsnorm(z[:, :, :, 0], q_gain)
    k = rmsnorm(z[:, :, :, 1], k_gain)
    v = z[:, :, :, 2]
    outs, lses = [], []
    for g, (window, dilation) in enumerate(DIL_PATTERNS):
        o_g, lse_g = dilated_branch(q[:, :, g], k[:, :, g], v[:, :, g], dilation, window // dilation)
        outs.append(o_g)
        lses.append(lse_g)
    wts = jax.nn.softmax(jnp.stack(lses, axis=0), axis=0)
    o = jnp.sum(wts[..., None].astype(v.dtype) * jnp.stack(outs, axis=0), axis=0)
    return o.reshape(B, S, ODD_MIX) @ w_out

def conv_ffn(h, w_up, conv_w, conv_b, w_down):
    u = h @ w_up
    u = lax.conv_general_dilated(u, conv_w, window_strides=(1,), padding=[(CONV_W - 1, 0)],
                                 dimension_numbers=('NWC', 'WIO', 'NWC'),
                                 feature_group_count=2 * D_FF) + conv_b
    gate, val = jnp.split(u, 2, axis=-1)
    return (jax.nn.silu(gate) * val) @ w_down

def first_inputs(seed: int = 0) -> dict:
    key = jax.random.key(seed)
    ks = iter(jax.random.split(key, 32))
    nrm = lambda shape, scale: jax.random.normal(next(ks), shape, jnp.float32) * scale
    gain = lambda shape: 1.0 + nrm(shape, 0.02)
    return {
        "x": nrm((BATCH, SEQ, D_MODEL), 1.0),
        "norm_mix": gain((DEPTH, D_MODEL)),
        "norm_ffn": gain((DEPTH, D_MODEL)),
        "ev_w_in": nrm((N_EVEN, D_MODEL, EVEN_IN), D_MODEL ** -0.5),
        "ev_w_a2": nrm((N_EVEN, GLA_RANK, A_QK), GLA_RANK ** -0.5),
        "ev_b_a": nrm((N_EVEN, A_QK), 0.1),
        "ev_gla_gain": gain((N_EVEN, GLA_DV)),
        "ev_dq_gain": gain((N_EVEN, DIFF_DH)),
        "ev_dk_gain": gain((N_EVEN, DIFF_DH)),
        "ev_lq1": nrm((N_EVEN, DIFF_DH), 0.1),
        "ev_lk1": nrm((N_EVEN, DIFF_DH), 0.1),
        "ev_lq2": nrm((N_EVEN, DIFF_DH), 0.1),
        "ev_lk2": nrm((N_EVEN, DIFF_DH), 0.1),
        "ev_diff_gain": gain((N_EVEN, DIFF_DV)),
        "ev_w_out": nrm((N_EVEN, EVEN_MIX, D_MODEL), EVEN_MIX ** -0.5),
        "od_w_in": nrm((N_ODD, D_MODEL, ODD_IN), D_MODEL ** -0.5),
        "od_q_gain": gain((N_ODD, DIL_DH)),
        "od_k_gain": gain((N_ODD, DIL_DH)),
        "od_w_out": nrm((N_ODD, ODD_MIX, D_MODEL), ODD_MIX ** -0.5),
        "ffn_w_up": nrm((DEPTH, D_MODEL, 2 * D_FF), D_MODEL ** -0.5),
        "ffn_conv_w": nrm((DEPTH, CONV_W, 1, 2 * D_FF), CONV_W ** -0.5),
        "ffn_conv_b": nrm((DEPTH, 2 * D_FF), 0.01),
        "ffn_w_down": nrm((DEPTH, D_FF, D_MODEL), D_FF ** -0.5),
    }

def first_block(x, norm_mix, norm_ffn, ev_w_in, ev_w_a2, ev_b_a, ev_gla_gain, ev_dq_gain, ev_dk_gain,
              ev_lq1, ev_lk1, ev_lq2, ev_lk2, ev_diff_gain, ev_w_out, od_w_in, od_q_gain, od_k_gain,
              od_w_out, ffn_w_up, ffn_conv_w, ffn_conv_b, ffn_w_down):
    for i in range(DEPTH):
        h = rmsnorm(x, norm_mix[i])
        if i % 2 == 0:
            e = i // 2
            lambda_init = 0.8 - 0.6 * math.exp(-0.3 * i)
            x = x + even_mixer(h, ev_w_in[e], ev_w_a2[e], ev_b_a[e], ev_gla_gain[e], ev_dq_gain[e],
                               ev_dk_gain[e], ev_lq1[e], ev_lk1[e], ev_lq2[e], ev_lk2[e],
                               ev_diff_gain[e], ev_w_out[e], lambda_init)
        else:
            o = i // 2
            x = x + odd_mixer(h, od_w_in[o], od_q_gain[o], od_k_gain[o], od_w_out[o])
        x = x + conv_ffn(rmsnorm(x, norm_ffn[i]), ffn_w_up[i], ffn_conv_w[i], ffn_conv_b[i], ffn_w_down[i])
    return x


GRID_W = 64
CTX_LEN = 256
HEAD_DIM = 64
ATTN_WIDTH = D_MODEL // 2
N_Q_HEADS = ATTN_WIDTH // HEAD_DIM
N_KV_HEADS = 2
Q_GROUP = N_Q_HEADS // N_KV_HEADS
KV_WIDTH = N_KV_HEADS * HEAD_DIM
ATTN_SCALE = HEAD_DIM ** -0.5
ROPE_THETA = 10000.0
POOL_WINDOWS = (2, 4, 8, 16)
POOL_WIDTH = D_MODEL - ATTN_WIDTH
POOL_GROUP_DIM = POOL_WIDTH // len(POOL_WINDOWS)
IN_A_WIDTH = ATTN_WIDTH + 2 * KV_WIDTH + POOL_WIDTH
OUT_A_WIDTH = ATTN_WIDTH + POOL_WIDTH
CHUNK = 128
GMLP_WIDTH = D_MODEL
GMLP_GROUPS = 8
GMLP_GROUP_DIM = GMLP_WIDTH // GMLP_GROUPS
N_MOD = 9
N_EVEN_2 = (DEPTH + 1) // 2
N_ODD_2 = DEPTH // 2


def rms_norm(x, g):
    xf = x.astype(jnp.float32)
    y = xf * lax.rsqrt(jnp.mean(xf * xf, axis=-1, keepdims=True) + EPS)
    return (y * g.astype(jnp.float32)).astype(x.dtype)

def modulate(x, g, shift, scale):
    return rms_norm(x, g) * (1 + scale) + shift

def swiglu(h, w13, w2):
    a, b = jnp.split(h @ w13, 2, axis=-1)
    return (jax.nn.silu(a) * b) @ w2

def half_ffn(x, g, shift, scale, gate, w13, w2):
    return x + 0.5 * gate * swiglu(modulate(x, g, shift, scale), w13, w2)

def axial_rope_tables(n_tokens, dtype):
    n_rows = n_tokens // GRID_W
    rows = jnp.repeat(jnp.arange(n_rows), GRID_W).astype(jnp.float32)
    cols = jnp.tile(jnp.arange(GRID_W), n_rows).astype(jnp.float32)
    half = HEAD_DIM // 2
    inv_freq = ROPE_THETA ** (-jnp.arange(0, half, 2, dtype=jnp.float32) / half)
    ang_r = rows[:, None] * inv_freq[None, :]
    ang_c = cols[:, None] * inv_freq[None, :]
    return (jnp.cos(ang_r).astype(dtype), jnp.sin(ang_r).astype(dtype),
            jnp.cos(ang_c).astype(dtype), jnp.sin(ang_c).astype(dtype))

def rope_half(x, cos, sin):
    x1, x2 = jnp.split(x, 2, axis=-1)
    cos = cos[None, :, None, :]
    sin = sin[None, :, None, :]
    return jnp.concatenate([x1 * cos - x2 * sin, x1 * sin + x2 * cos], axis=-1)

def apply_axial_rope(x, tabs):
    cr, sr, cc, sc = tabs
    xr, xc = jnp.split(x, 2, axis=-1)
    return jnp.concatenate([rope_half(xr, cr, sr), rope_half(xc, cc, sc)], axis=-1)

def gqa_attend(q, k, v):
    b, nq = q.shape[:2]
    qg = q.reshape(b, nq, N_KV_HEADS, Q_GROUP, HEAD_DIM)
    sc = jnp.einsum('bqhgd,bkhd->bhgqk', qg, k, preferred_element_type=jnp.float32) * ATTN_SCALE
    pr = jax.nn.softmax(sc, axis=-1).astype(v.dtype)
    return jnp.einsum('bhgqk,bkhd->bqhgd', pr, v).reshape(b, nq, ATTN_WIDTH)

def latent_attention(q, k_lat, v_lat, k_ctx, v_ctx):
    b, s = q.shape[:2]
    k_all = jnp.concatenate([k_ctx, k_lat], axis=1)
    v_all = jnp.concatenate([v_ctx, v_lat], axis=1)
    nb = s // Q_BLOCK
    qb = jnp.moveaxis(q.reshape(b, nb, Q_BLOCK, N_Q_HEADS, HEAD_DIM), 1, 0)
    ob = lax.map(lambda qblk: gqa_attend(qblk, k_all, v_all), qb)
    return jnp.moveaxis(ob, 0, 1).reshape(b, s, ATTN_WIDTH)

def project_a(h, w_in, qk_g):
    b, n = h.shape[:2]
    z = h @ w_in
    q = rms_norm(z[..., :ATTN_WIDTH].reshape(b, n, N_Q_HEADS, HEAD_DIM), qk_g[0])
    k = rms_norm(z[..., ATTN_WIDTH:ATTN_WIDTH + KV_WIDTH].reshape(b, n, N_KV_HEADS, HEAD_DIM), qk_g[1])
    v = z[..., ATTN_WIDTH + KV_WIDTH:ATTN_WIDTH + 2 * KV_WIDTH].reshape(b, n, N_KV_HEADS, HEAD_DIM)
    p = z[..., ATTN_WIDTH + 2 * KV_WIDTH:]
    return q, k, v, p

def project_ctx_kv(h, w_in, qk_g):
    b, n = h.shape[:2]
    z = h @ w_in[:, ATTN_WIDTH:ATTN_WIDTH + 2 * KV_WIDTH]
    k = rms_norm(z[..., :KV_WIDTH].reshape(b, n, N_KV_HEADS, HEAD_DIM), qk_g[1])
    v = z[..., KV_WIDTH:].reshape(b, n, N_KV_HEADS, HEAD_DIM)
    return k, v

def multiscale_pool(p, pool_w, pool_scale):
    n = p.shape[1]
    pf = p.astype(jnp.float32)
    cs = jnp.concatenate([jnp.zeros_like(pf[:, :1]), jnp.cumsum(pf, axis=1)], axis=1)
    t = jnp.arange(n)
    outs = []
    for gi, w in enumerate(POOL_WINDOWS):
        sl = slice(gi * POOL_GROUP_DIM, (gi + 1) * POOL_GROUP_DIM)
        lo = jnp.clip(t - w // 2, 0, n)
        hi = jnp.clip(t + w // 2, 0, n)
        csg = cs[..., sl]
        mean = (csg[:, hi] - csg[:, lo]) / (hi - lo).astype(jnp.float32)[None, :, None]
        outs.append((mean - pf[..., sl]).astype(p.dtype) @ pool_w[gi])
    return jnp.concatenate(outs, axis=-1) * pool_scale

def combine_a(attn, p, pool_w, pool_scale, w_out):
    return jnp.concatenate([attn, multiscale_pool(p, pool_w, pool_scale)], axis=-1) @ w_out

def mixer_c(h, w_in, v_g, w_sp, b_sp, w_out):
    b, n = h.shape[:2]
    z = jax.nn.gelu(h @ w_in)
    u, v = jnp.split(z, 2, axis=-1)
    v = rms_norm(v, v_g)
    vc = v.reshape(b, n // CHUNK, CHUNK, GMLP_GROUPS, GMLP_GROUP_DIM)
    sv = jnp.einsum('gpq,bnqgc->bnpgc', w_sp, vc) + b_sp.T[None, None, :, :, None]
    return (u * sv.reshape(b, n, GMLP_WIDTH)) @ w_out

def second_inputs(seed: int = 0) -> dict:
    key = jax.random.key(seed)
    ks = jax.random.split(key, 20)
    f32 = jnp.float32

    def nrm(k, shape, fan_in):
        return jax.random.normal(k, shape, f32) * (fan_in ** -0.5)

    def gain(k, shape):
        return 1.0 + 0.05 * jax.random.normal(k, shape, f32)

    return {
        "x": jax.random.normal(ks[0], (BATCH, SEQ, D_MODEL), f32),
        "c": jax.random.normal(ks[1], (BATCH, D_MODEL), f32),
        "ctx": jax.random.normal(ks[2], (BATCH, CTX_LEN, D_MODEL), f32),
        "c_ctx": jax.random.normal(ks[3], (D_MODEL,), f32),
        "w_mod": 0.5 * nrm(ks[4], (DEPTH, D_MODEL, N_MOD * D_MODEL), D_MODEL),
        "b_mod": 0.01 * jax.random.normal(ks[5], (DEPTH, N_MOD * D_MODEL), f32),
        "norm_g": gain(ks[6], (DEPTH, 3, D_MODEL)),
        "ffn_w13": nrm(ks[7], (DEPTH, 2, D_MODEL, 2 * D_FF), D_MODEL),
        "ffn_w2": nrm(ks[8], (DEPTH, 2, D_FF, D_MODEL), D_FF),
        "w_in_a": nrm(ks[9], (N_EVEN_2, D_MODEL, IN_A_WIDTH), D_MODEL),
        "qk_norm_g": gain(ks[10], (N_EVEN_2, 2, HEAD_DIM)),
        "pool_w": nrm(ks[11], (N_EVEN_2, len(POOL_WINDOWS), POOL_GROUP_DIM, POOL_GROUP_DIM), POOL_GROUP_DIM),
        "pool_scale": gain(ks[12], (N_EVEN_2, POOL_WIDTH)),
        "w_out_a": nrm(ks[13], (N_EVEN_2, OUT_A_WIDTH, D_MODEL), OUT_A_WIDTH),
        "w_in_c": nrm(ks[14], (N_ODD_2, D_MODEL, 2 * GMLP_WIDTH), D_MODEL),
        "v_norm_g": gain(ks[15], (N_ODD_2, GMLP_WIDTH)),
        "w_sp": nrm(ks[16], (N_ODD_2, GMLP_GROUPS, CHUNK, CHUNK), CHUNK),
        "b_sp": gain(ks[17], (N_ODD_2, GMLP_GROUPS, CHUNK)),
        "w_out_c": nrm(ks[18], (N_ODD_2, GMLP_WIDTH, D_MODEL), GMLP_WIDTH),
    }

def second_block(x, c, ctx, c_ctx, w_mod, b_mod, norm_g, ffn_w13, ffn_w2,
              w_in_a, qk_norm_g, pool_w, pool_scale, w_out_a,
              w_in_c, v_norm_g, w_sp, b_sp, w_out_c):
    b, s, d = x.shape
    rope_tabs = axial_rope_tables(s, x.dtype)
    silu_c = jax.nn.silu(c)
    silu_cc = jax.nn.silu(c_ctx)
    cs = ctx
    for i in range(DEPTH):
        m = (silu_c @ w_mod[i] + b_mod[i]).reshape(b, 1, N_MOD, d)
        reads_ctx = (i % 2 == 0)
        later_reads_ctx = any(j % 2 == 0 for j in range(i + 1, DEPTH))
        ctx_needed = reads_ctx or later_reads_ctx
        if ctx_needed:
            mc = (silu_cc @ w_mod[i] + b_mod[i]).reshape(1, 1, N_MOD, d)
            cs = half_ffn(cs, norm_g[i, 0], mc[:, :, 0], mc[:, :, 1], mc[:, :, 2],
                          ffn_w13[i, 0], ffn_w2[i, 0])
        x = half_ffn(x, norm_g[i, 0], m[:, :, 0], m[:, :, 1], m[:, :, 2], ffn_w13[i, 0], ffn_w2[i, 0])

        h = modulate(x, norm_g[i, 1], m[:, :, 3], m[:, :, 4])
        if i % 2 == 0:
            e = i // 2
            hc = modulate(cs, norm_g[i, 1], mc[:, :, 3], mc[:, :, 4])
            if later_reads_ctx:
                qc, kc, vc, pc = project_a(hc, w_in_a[e], qk_norm_g[e])
            else:
                kc, vc = project_ctx_kv(hc, w_in_a[e], qk_norm_g[e])
            q, k, v, p = project_a(h, w_in_a[e], qk_norm_g[e])
            q = apply_axial_rope(q, rope_tabs)
            k = apply_axial_rope(k, rope_tabs)
            attn = latent_attention(q, k, v, kc, vc)
            x = x + m[:, :, 5] * combine_a(attn, p, pool_w[e], pool_scale[e], w_out_a[e])
            if later_reads_ctx:
                attn_c = gqa_attend(qc, kc, vc)
                cs = cs + mc[:, :, 5] * combine_a(attn_c, pc, pool_w[e], pool_scale[e], w_out_a[e])
        else:
            o = i // 2
            x = x + m[:, :, 5] * mixer_c(h, w_in_c[o], v_norm_g[o], w_sp[o], b_sp[o], w_out_c[o])
            if later_reads_ctx:
                hc = modulate(cs, norm_g[i, 1], mc[:, :, 3], mc[:, :, 4])
                cs = cs + mc[:, :, 5] * mixer_c(hc, w_in_c[o], v_norm_g[o], w_sp[o], b_sp[o], w_out_c[o])

        if later_reads_ctx:
            cs = half_ffn(cs, norm_g[i, 2], mc[:, :, 6], mc[:, :, 7], mc[:, :, 8],
                          ffn_w13[i, 1], ffn_w2[i, 1])
        x = half_ffn(x, norm_g[i, 2], m[:, :, 6], m[:, :, 7], m[:, :, 8], ffn_w13[i, 1], ffn_w2[i, 1])
    return x


def setup_inputs(seed=0):
    out = dict(first_inputs(seed))
    for name, value in second_inputs(seed + 1).items():
        if name != "x":
            out[name + "_2"] = value
    return out


def reference(
    x, norm_mix, norm_ffn, ev_w_in, ev_w_a2, ev_b_a, ev_gla_gain, ev_dq_gain, ev_dk_gain,
    ev_lq1, ev_lk1, ev_lq2, ev_lk2, ev_diff_gain, ev_w_out, od_w_in, od_q_gain, od_k_gain,
    od_w_out, ffn_w_up, ffn_conv_w, ffn_conv_b, ffn_w_down, c_2, ctx_2, c_ctx_2, w_mod_2,
    b_mod_2, norm_g_2, ffn_w13_2, ffn_w2_2, w_in_a_2, qk_norm_g_2, pool_w_2, pool_scale_2,
    w_out_a_2, w_in_c_2, v_norm_g_2, w_sp_2, b_sp_2, w_out_c_2,
):
    x = first_block(
        x, norm_mix, norm_ffn, ev_w_in, ev_w_a2, ev_b_a, ev_gla_gain, ev_dq_gain, ev_dk_gain,
        ev_lq1, ev_lk1, ev_lq2, ev_lk2, ev_diff_gain, ev_w_out, od_w_in, od_q_gain, od_k_gain,
        od_w_out, ffn_w_up, ffn_conv_w, ffn_conv_b, ffn_w_down,
    )
    return second_block(
        x, c_2, ctx_2, c_ctx_2, w_mod_2, b_mod_2, norm_g_2, ffn_w13_2, ffn_w2_2, w_in_a_2,
        qk_norm_g_2, pool_w_2, pool_scale_2, w_out_a_2, w_in_c_2, v_norm_g_2, w_sp_2, b_sp_2,
        w_out_c_2,
    )


_drawn_inputs = setup_inputs


def setup_inputs(seed=0):
    import zlib

    import numpy as np

    out = dict(_drawn_inputs(seed))
    spreads = {}
    factors = {'norm_ffn': 2.999,
     'ev_b_a': 2.961,
     'ev_gla_gain': 6.311,
     'ev_dq_gain': 4.566,
     'ev_dk_gain': 4.969,
     'ev_lq1': 6.184,
     'ev_lk1': 8.0,
     'ev_diff_gain': 4.793,
     'od_q_gain': 8.0,
     'od_k_gain': 8.0,
     'ffn_conv_b': 6.192,
     'ctx_2': 8.0,
     'c_ctx_2': 4.253,
     'b_mod_2': 5.589,
     'norm_g_2': 3.245,
     'qk_norm_g_2': 8.0,
     'pool_scale_2': 8.0,
     'v_norm_g_2': 21.575,
     'b_sp_2': 31.081,
     'ev_lq2': 8.0,
     'ev_lk2': 8.0}
    for name, (base, spread) in spreads.items():
        noise = np.random.default_rng([zlib.crc32(name.encode()), seed]).standard_normal(out[name].shape)
        drawn = base * np.exp(spread * noise) if base else spread * noise
        out[name] = __import__('jax').numpy.asarray(drawn.astype(out[name].dtype))
    for name, factor in factors.items():
        out[name] = (out[name] * factor).astype(out[name].dtype)
    return out
```

```python
from contextlib import ExitStack

import numpy as np
import concourse.bass as bass
from concourse import mybir

F32 = mybir.dt.float32
F32R = mybir.dt.float32r
U32 = mybir.dt.uint32
ALU = mybir.AluOpType
ACT = mybir.ActivationFunctionType
AX_X = mybir.AxisListType.X

P = 128
D = 1024
DC = D // P
S = 512
TT = S // P
CTX = 256
FF = 2816
FC = FF // P
SLAB = 2048
WPOOL = 512
GROUPS = [(0, 8), (8, 16), (16, FC)]
EPS = 1e-6
N_MOD = 9
DIL = (1, 4, 16)
POOL_WINDOWS = (2, 4, 8, 16)

PLAN = {}
_n = 0
for _name, _k in [("mod", 72), ("ctx_ffn", 34), ("ctx_kv", 1), ("even_in", 13), ("even_out", 4), ("conv0", 34),
                  ("odd_in0", 9), ("odd_in1", 9), ("odd_out", 4), ("conv1", 34), ("ffn00", 34), ("a_in", 5),
                  ("a_out", 4), ("ffn01", 34), ("ffn10", 34), ("c_in", 8), ("c_out", 4), ("ffn11", 34)]:
    PLAN[_name] = (_n, _k)
    _n += _k
NSLAB = _n

ROUND = {}
for _name, _k in [("ctx_ffn", 3), ("even", 1), ("conv0", 3), ("odd", 1), ("conv1", 3), ("ffn00", 3), ("a", 1),
                  ("ffn01", 3), ("ffn10", 3), ("c", 1), ("ffn11", 3)]:
    for _j in range(_k):
        ROUND[_name, _j] = len(ROUND)

NORM = {n: i for i, n in enumerate(["ctx0", "ctx1", "mix0", "cffn0", "mix1", "cffn1", "m00", "m01", "m02", "m10",
                                    "m11", "m12"])}
NORM_ROUND = {"ctx0": None, "ctx1": ("ctx_ffn", 2), "mix0": None, "cffn0": ("even", 0), "mix1": ("conv0", 2),
              "cffn1": ("odd", 0), "m00": ("conv1", 2), "m01": ("ffn00", 2), "m02": ("a", 0), "m10": ("ffn01", 2),
              "m11": ("ffn10", 2), "m12": ("c", 0)}

SPLIT = {}
_n = 0
for _name, _k in [("ctx0", 8), ("ctx_ffn", FC), ("ctx1", 8), ("mix0", 8), ("even", 8), ("cffn0", 8), ("conv0", FC),
                  ("mix1", 8), ("odd", 4), ("cffn1", 8), ("conv1", FC), ("m00", 8), ("ffn00", FC), ("m01", 8),
                  ("a", 8), ("m02", 8), ("ffn01", FC), ("m10", 8), ("ffn10", FC), ("m11", 8), ("c", 8), ("m12", 8),
                  ("ffn11", FC)]:
    SPLIT[_name] = (_n, _k)
    _n += _k

PC = {}
_n = 0
for _name, _k in [("eps", 1), ("norm_mix", 16), ("norm_ffn", 16), ("conv_w", 2 * 3 * 2 * FC), ("conv_b", 2 * 2 * FC),
                  ("norm_g", 48), ("b_mod", 144), ("b_a", 2), ("gla_gain", 1), ("dq_gain", 1), ("dk_gain", 1),
                  ("diff_gain", 1), ("lam4", 4), ("odq", 1), ("odk", 1), ("qkn", 2), ("pool_scale", 4),
                  ("v_norm", 8), ("c2", 16)]:
    PC[_name] = _n
    _n += _k
NPAR = _n

KC_IDENT, KC_M1024, KC_M128, KC_M64, KC_CAUSAL, KC_ONES, KC_COMB = 0, 128, 256, 384, 512, 640, 768
NKEEP = 770
KE_GLA, KE_SCAN, NEVEN = 0, 128, 640
KO_NEAR, KO_G1, KO_G2, NODD = 0, 2048, 2176, 2304
KA_ROT, KA_COS, KA_SIN, KA_CNT, NA = 0, 128, 640, 1152, 1152 + 2048
NEG = -1e30
LAMBDA_INIT = 0.2

SILU_CH = {n: FC * i for i, n in enumerate(["ctx_ffn", "conv0", "conv1", "ffn00", "ffn01", "ffn10", "ffn11"])}
CONV_CH = {"conv0": 0, "conv1": FC}


def build(nc, stream, params, xT, ctxT, keep, k_even, k_odd, k_a, w_a2, pool_w, w_spT, b_sp, out):
    def ts(i, n):
        return bass.ts(i, n)

    with ExitStack() as es:
        def sb(name, shape, dt=F32):
            return es.enter_context(nc.sbuf_tensor(name, shape, dt))

        def sem(name):
            return es.enter_context(nc.semaphore(name))

        x = sb("x", [P, DC, S])
        h_hi = sb("h_hi", [P, DC, S], F32R)
        h_lo = sb("h_lo", [P, DC, S], F32R)
        raw = sb("raw", [P, 2, SLAB])
        whi = sb("whi", [P, 2, SLAB], F32R)
        wlo = sb("wlo", [P, 2, SLAB], F32R)
        stg = sb("stg", [P, 2, S])
        sq = sb("sq", [P, 2, S])
        rstd = sb("rstd", [P, 2, S])
        par = sb("par", [P, NPAR])
        kp = sb("kp", [P, NKEEP])
        modT = sb("modT", [P, 144, 2])
        modA = sb("modA", [P, 8, 8])
        gates = sb("gates", [P, 7, 8])
        kctx = sb("kctx", [P, CTX])
        vctx = sb("vctx", [P, 2, P])
        small = sb("small", [P, 64])
        ident = kp[:, KC_IDENT:KC_IDENT + P]
        causal = kp[:, KC_CAUSAL:KC_CAUSAL + P]
        ones = kp[:, KC_ONES:KC_ONES + P]
        mean_of = {D: kp[:, KC_M1024:KC_M1024 + P], 128: kp[:, KC_M128:KC_M128 + P], 64: kp[:, KC_M64:KC_M64 + P]}

        def scope(tensors):
            made = []
            with ExitStack() as own:
                for name, shape, *dt in tensors:
                    made.append(own.enter_context(nc.sbuf_tensor(name, shape, dt[0] if dt else F32)))
            return made

        mid_hi, mid_lo, cg, cv, sg = scope([
            ("mid_hi", [P, 2, 8, S], F32R), ("mid_lo", [P, 2, 8, S], F32R),
            ("cg", [P, 2, S]), ("cv", [P, 2, S]), ("sg", [P, 2, S])])
        cT, csil, modrow = scope([("cT", [P, DC, P], F32R), ("csil", [P, 16]), ("modrow", [4, 2, 256])])
        (aq, ak, sag, bq, bk, av, bv, arT, wa2, ke, gt, decay, attm, gb, kk, kkT, gst) = scope([
            ("aq", [P, 2, S]), ("ak", [P, 2, S]), ("sag", [P, 4, S]), ("bq", [P, 4, S]), ("bk", [P, 4, S]),
            ("av", [P, TT, S]), ("bv", [P, TT, S]), ("arT", [16, S]), ("wa2", [16, 256]), ("ke", [P, NEVEN]),
            ("gt", [P, 4, S]), ("decay", [P, 2, 8]), ("attm", [P, 2, S]), ("gb", [P, 2, S]), ("kk", [P, 2, S]),
            ("kkT", [P, 2, S]), ("gst", [P, 2, 7, P])])
        _, *dtmp = scope([("below", [P, 24 * S + S + 256 + NEVEN + 4 * S + 16 + 2 * S]),
                          ("dP", [P, 2, 2 * S]), ("dW", [P, 2, S]), ("dWT", [P, 2, S])])
        oq, okk, ov, ko, oP, oW, oWT, oo = scope([
            ("oq", [P, 6, S]), ("okk", [P, 6, S]), ("ov", [P, 3, TT, 256]), ("ko", [P, NODD]),
            ("oP", [P, 2, 768]), ("oW", [P, 2, 768]), ("oWT", [P, 2, 768]), ("oo", [P, 4, S])])
        qa, kall, vall, pp, pa, pb, pd, ka, wpool, rot, aP, aW, aWT = scope([
            ("qa", [P, 4, S]), ("kall", [P, CTX + S]), ("vall", [P, 6, P]), ("pp", [P, 4, 16 + S]),
            ("pa", [P, 16 + S]), ("pb", [P, 16 + S]), ("pd", [P, 4, S]), ("ka", [P, NA]), ("wpool", [P, 4, P]),
            ("rot", [P, 2, S]), ("aP", [P, 2, 768]), ("aW", [P, 2, 768]), ("aWT", [P, 2, 768])])
        u, vt, wsp, bsp, sv, vss = scope([
            ("u", [P, 8, S]), ("vt", [P, TT, D]), ("wsp", [P, 8, P]), ("bsp", [P, 8, P]), ("sv", [P, 2, S]),
            ("vss", [P, 16])])

        bank = [es.enter_context(nc.psum_tensor(f"bank{i}", [P, 512], F32)) for i in range(8)]
        acc = [[bank[0], bank[1]], [bank[2], bank[3]]]
        aux = bank[4:8]

        raw_loaded = [sem("raw_loaded0"), sem("raw_loaded1")]
        whi_done = sem("whi_done")
        wlo_done = sem("wlo_done")
        wlo_pool_done = sem("wlo_pool_done")
        slab_done = sem("slab_done")
        stg_ready = sem("stg_ready")
        hi_done = sem("hi_done")
        lo_done = sem("lo_done")
        x_written = sem("x_written")
        x_loaded = sem("x_loaded")
        par_loaded = sem("par_loaded")
        stage_loaded = sem("stage_loaded")
        sq_ready = sem("sq_ready")
        stat_done = sem("stat_done")
        rstd_ready = sem("rstd_ready")
        dve_step = sem("dve_step")
        act_step = sem("act_step")
        pool_step = sem("pool_step")
        tap_done = sem("tap_done")
        center_done = sem("center_done")
        silu_done = sem("silu_done")
        modrow_ready = sem("modrow_ready")
        modcol_ready = sem("modcol_ready")
        modcol_used = sem("modcol_used")
        mod_done = sem("mod_done")
        csil_ready = sem("csil_ready")
        cT_ready = sem("cT_ready")
        cT_lo = sem("cT_lo")
        small_ready = sem("small_ready")
        stored = sem("stored")

        def att_sems(n):
            return {k: sem(f"{n}_{k}") for k in ("scores", "negmax", "probs", "weights", "turned", "copied", "mixed",
                                                 "taken")}

        def hn_sems(n):
            return {k: sem(f"{n}_{k}") for k in ("sq", "stat", "rstd", "out")}

        sem_diff, sem_odd, sem_a = att_sems("diff"), att_sems("odd"), att_sems("rope")
        hn = hn_sems("hn")
        HN = {}
        n = 0
        for name, k in [("ctx", 1), ("gla", 4), ("qk", 8), ("diff", 4), ("odd0", 12), ("odd1", 12), ("a", 5)]:
            HN[name] = (n, k)
            n += k
        gla = {k: sem(f"gla_{k}") for k in ("la", "abs", "b", "eb", "kk", "turned", "copied", "kv", "state", "att",
                                            "masked", "out", "taken", "lastdiff")}
        lam_sem = {k: sem(f"lam_{k}") for k in ("prod", "sum", "exp")}
        rope = {k: sem(f"rope_{k}") for k in ("rot", "done")}
        poolm = {k: sem(f"poolm_{k}") for k in ("diff", "mixed")}
        cmix = {k: sem(f"cmix_{k}") for k in ("u", "ss", "rs", "v", "mixed", "sv")}

        DIFF_U = [(hd, t) for hd in range(4) for t in range(TT)]
        ODD_U = [(hh, r) for hh in range(2) for r in range(4)]
        A_U = [(hd, t) for hd in range(8) for t in range(TT)]

        def slab_of(name, i=0):
            return PLAN[name][0] + i

        def needs_round(e, norm, c):
            r = NORM_ROUND[norm]
            if r is None:
                e.wait_ge(x_loaded, 16 if norm == "ctx0" else 32)
            else:
                e.wait_ge(x_written, 8 * ROUND[r] + c + 1)

        def projections_taken(e, name):
            end = PLAN[name][0] + PLAN[name][1]
            e.wait_ge(whi_done, end + 2)
            e.wait_ge(wlo_done, end + 2)

        block = es.enter_context(nc.Block())

        @block.sync
        def _(sp):
            sp.dma_start(par[:], params).then_inc(par_loaded, 16)
            sp.dma_start(kp[:], keep).then_inc(par_loaded, 16)
            for s in range(2):
                sp.dma_start(raw[:, s, :], stream[s]).then_inc(raw_loaded[s], 16)
            sp.dma_start(x[:, :, 0:CTX], ctxT.rearrange("(c p) t -> p c t", p=P)).then_inc(x_loaded, 16)

            def load(s, slot, at):
                sp.wait_ge(wlo_done, s - 1)
                sp.wait_ge(wlo_pool_done, s - 1)
                sp.dma_start(raw[:, slot, :], at).then_inc(raw_loaded[slot], 16)

            def loads(a, b):
                with sp.Fori(0, (b - a) // 2) as i:
                    for j in range(2):
                        load(a + j + 2 * i, (a + j) % 2,
                             stream[bass.ds(a + j + 2 * i, 1), :, :].rearrange("a p n -> (a p) n"))

            first = PLAN["ctx_kv"][0] + 2
            loads(2, first)
            sp.wait_ge(lo_done, SPLIT["ctx1"][0] + 8)
            sp.wait_ge(hi_done, SPLIT["ctx1"][0] + 8)
            sp.dma_start(x[:], xT.rearrange("(c p) t -> p c t", p=P)).then_inc(x_loaded, 16)
            even_n = (NSLAB - first) // 2 * 2
            loads(first, first + even_n)
            for s in range(first + even_n, NSLAB):
                load(s, s % 2, stream[s])
            sp.wait_ge(x_written, 8 * (ROUND["ffn11", 2] + 1))
            sp.dma_start(out.rearrange("(c p) t -> p c t", p=P), x[:]).then_inc(stored, 16)
            sp.wait_ge(stored, 16)

        @block.tensor
        def _(pe):
            mm = nc.tensor.matmul

            def slab_split(s):
                pe.wait_ge(whi_done, s + 1)
                pe.wait_ge(wlo_done, s + 1)
                pe.wait_ge(wlo_pool_done, s + 1)

            def w_tile(w, slot, kc, j, n=P):
                return w[:, slot, kc * 256 + j * P:kc * 256 + j * P + n]

            def slab_out(s, slot, a_hi, a_lo, K, T, js=(0, 1), split0=None):
                slab_split(s)
                for kc in range(K):
                    if split0 is not None:
                        pe.wait_ge(hi_done, split0 + kc + 1)
                        pe.wait_ge(lo_done, split0 + kc + 1)
                    for j in js:
                        o = acc[slot][j][:, 0:T]
                        hi, lo = w_tile(whi, slot, kc, j), w_tile(wlo, slot, kc, j)
                        mm(o, hi, a_hi[:, kc, 0:T], start=(kc == 0), stop=False)
                        mm(o, hi, a_lo[:, kc, 0:T], start=False, stop=False)
                        last = mm(o, lo, a_hi[:, kc, 0:T], start=False, stop=(kc == K - 1))
                last.then_inc(slab_done, 1)

            def slab_tokens(s, slot, tiles, col0=0, ncol=256):
                slab_split(s)
                for i, tok in enumerate(tiles):
                    o = acc[slot][i // 2][:, 256 * (i % 2):256 * (i % 2) + ncol]
                    for kc in range(DC):
                        w_h = whi[:, slot, kc * 256 + col0:kc * 256 + col0 + ncol]
                        w_l = wlo[:, slot, kc * 256 + col0:kc * 256 + col0 + ncol]
                        a_h, a_l = h_hi[:, kc, tok], h_lo[:, kc, tok]
                        mm(o, a_h, w_h, start=(kc == 0), stop=False)
                        mm(o, a_l, w_h, start=False, stop=False)
                        last = mm(o, a_h, w_l, start=False, stop=(kc == DC - 1))
                last.then_inc(slab_done, 1)

            def slabs(s0, n, a_hi, a_lo, K, T, split0=None):
                peel = min(2, n) if split0 is not None else 0
                for i in range(peel):
                    slab_out(s0 + i, (s0 + i) % 2, a_hi, a_lo, K, T, split0=split0 if i == 0 else None)
                if (n - peel) // 2 > 1:
                    with pe.Fori(0, (n - peel) // 2) as i:
                        for j in range(2):
                            s = s0 + peel + j
                            slab_out(s + 2 * i, s % 2, a_hi, a_lo, K, T)
                    rest = s0 + peel + (n - peel) // 2 * 2
                else:
                    rest = s0 + peel
                for s in range(rest, s0 + n):
                    slab_out(s, s % 2, a_hi, a_lo, K, T)

            def stat(norm, c, T):
                n = 8 * NORM[norm] + c
                pe.wait_ge(sq_ready, n + 1)
                mm(aux[0][:, 0:T], mean_of[D], sq[:, n % 2, 0:T], start=(c == 0), stop=(c == 7)).then_inc(stat_done, 1)

            def slabs_and_stats(s0, a_hi, a_lo, K, T, norm, split0=None):
                for i in range(4):
                    slab_out(s0 + i, (s0 + i) % 2, a_hi, a_lo, K, T, split0=split0 if i == 0 else None)
                    if norm and i >= 1:
                        stat(norm, 2 * i - 2, T)
                        stat(norm, 2 * i - 1, T)
                if norm:
                    stat(norm, 6, T)
                    stat(norm, 7, T)

            def ffn(name, split_h, T, norm):
                s, n0 = slab_of(name), SPLIT[name][0]
                up = [(s, 8), (s + 8, 8), (s + 20, 6)]
                slabs(s, 8, h_hi, h_lo, DC, T, split0=SPLIT[split_h][0])
                slabs(s + 8, 8, h_hi, h_lo, DC, T)
                slabs(s + 16, 4, mid_hi[:, 0], mid_lo[:, 0], 8, T, split0=n0)
                slabs(s + 20, 6, h_hi, h_lo, DC, T)
                slabs(s + 26, 4, mid_hi[:, 1], mid_lo[:, 1], 8, T, split0=n0 + 8)
                slabs_and_stats(s + 30, mid_hi[:, 0], mid_lo[:, 0], 6, T, norm, split0=n0 + 16)

            def head_stats(name, srcs, width, ready, T=S):
                n0 = HN[name][0]
                for i in range(len(srcs)):
                    n = n0 + i
                    pe.wait_ge(hn["sq"], n + 1)
                    mm(aux[n % 2][:, 0:T], mean_of[width], sq[:, n % 2, 0:T], start=True, stop=True)\
                        .then_inc(hn["stat"], 1)

            def attention(sems, units, scores, nblocks, w_ap, wt_ap, mix):
                U = len(units)

                def turn(n):
                    pe.wait_ge(sems["weights"], n + 1)
                    if n >= 1:
                        pe.wait_ge(sems["copied"], n)
                    for b in range(nblocks(n)):
                        last = nc.tensor.transpose(aux[b // 4][:, (b % 4) * P:(b % 4) * P + P],
                                                   w_ap[:, n % 2, b * P:(b + 1) * P], ident)
                    last.then_inc(sems["turned"], 1)

                def score(n):
                    if n >= 2:
                        pe.wait_ge(sems["probs"], n - 1)
                    scores(n, acc[n % 2]).then_inc(sems["scores"], 1)

                score(0)
                score(1)
                for n in range(U):
                    turn(n)
                    if n + 2 < U:
                        score(n + 2)
                    pe.wait_ge(sems["copied"], n + 1)
                    mix(n).then_inc(sems["mixed"], 1)

            pe.wait_ge(par_loaded, 32)
            pe.wait_ge(cT_lo, 16)

            def mod_slab(s, slot):
                slab_split(s)
                o = acc[slot][0][:, 0:256]
                for kc in range(DC):
                    mm(o, cT[:, kc, :], whi[:, slot, kc * 256:kc * 256 + 256], start=(kc == 0), stop=False)
                    last = mm(o, cT[:, kc, :], wlo[:, slot, kc * 256:kc * 256 + 256], start=False, stop=(kc == 7))
                last.then_inc(slab_done, 1)

            def mod_turn(s, slot, first=False):
                pe.wait_ge(modrow_ready, s + 1)
                if not first:
                    pe.wait_ge(mod_done, s - 1)
                for j in range(2):
                    last = mm(aux[slot][:, 2 * j:2 * j + 2], modrow[0:4, slot, j * P:(j + 1) * P],
                              kp[0:4, KC_COMB:KC_COMB + 2], start=True, stop=True)
                last.then_inc(modcol_ready, 1)

            mod_slab(0, 0)
            mod_slab(1, 1)
            mod_turn(0, 0, first=True)
            mod_slab(2, 0)
            mod_turn(1, 1, first=True)
            with pe.Fori(0, 34) as i:
                mod_slab(3 + 2 * i, 1)
                mod_turn(2 + 2 * i, 0)
                mod_slab(4 + 2 * i, 0)
                mod_turn(3 + 2 * i, 1)
            mod_slab(71, 1)
            mod_turn(70, 0)
            mod_turn(71, 1)

            pe.wait_ge(mod_done, 72)
            for c in range(8):
                stat("ctx0", c, CTX)
            ffn("ctx_ffn", "ctx0", CTX, "ctx1")
            s = slab_of("ctx_kv")
            split0 = SPLIT["ctx1"][0]
            slab_split(s)
            pe.wait_ge(hi_done, split0 + 8)
            pe.wait_ge(lo_done, split0 + 8)
            slot = s % 2
            for kc in range(DC):
                o = acc[slot][0][:, 0:CTX]
                mm(o, w_tile(whi, slot, kc, 0), h_hi[:, kc, 0:CTX], start=(kc == 0), stop=False)
                mm(o, w_tile(whi, slot, kc, 0), h_lo[:, kc, 0:CTX], start=False, stop=False)
                mm(o, w_tile(wlo, slot, kc, 0), h_hi[:, kc, 0:CTX], start=False, stop=(kc == 7))
            for i in range(2):
                o = acc[slot][1][:, P * i:P * i + P]
                for kc in range(DC):
                    a_h, a_l = h_hi[:, kc, i * P:(i + 1) * P], h_lo[:, kc, i * P:(i + 1) * P]
                    mm(o, a_h, w_tile(whi, slot, kc, 1), start=(kc == 0), stop=False)
                    mm(o, a_l, w_tile(whi, slot, kc, 1), start=False, stop=False)
                    last = mm(o, a_h, w_tile(wlo, slot, kc, 1), start=False, stop=(kc == 7))
            last.then_inc(slab_done, 1)
            head_stats("ctx", [0], 64, None, CTX)

            for c in range(8):
                stat("mix0", c, S)
            s = slab_of("even_in")
            slab_out(s, s % 2, h_hi, h_lo, DC, S, js=(0,), split0=SPLIT["mix0"][0])
            slabs(s + 1, 8, h_hi, h_lo, DC, S)
            toks = [slice(t * P, (t + 1) * P) for t in range(TT)]
            for i in range(4):
                slab_tokens(s + 9 + i, (s + 9 + i) % 2, toks)
            projections_taken(pe, "even_in")
            pe.wait_ge(stage_loaded, 32)
            for p in range(2):
                mm(aux[p][:], wa2[:, p * P:(p + 1) * P], arT[:], start=True, stop=True).then_inc(gla["la"], 1)
            for p in range(2):
                pe.wait_ge(gla["kk"], p + 1)
                for t in range(TT):
                    last = nc.tensor.transpose(aux[2 + p][:, t * P:(t + 1) * P], kk[:, p, t * P:(t + 1) * P], ident)
                last.then_inc(gla["turned"], 1)
            pe.wait_ge(gla["copied"], 2)
            for n in range(7):
                t, half = n // 2, 64 * (n % 2)
                if n >= 4:
                    pe.wait_ge(gla["state"], 4 * (n - 3))
                for p in range(2):
                    last = mm(bank[n % 4][:, 256 * p:256 * p + 256], kkT[half:half + 64, p, t * P:(t + 1) * P],
                              av[half:half + 64, t, 256 * p:256 * p + 256], start=True, stop=True)
                last.then_inc(gla["kv"], 1)
            pe.wait_ge(gla["eb"], 4)
            pe.wait_ge(gla["abs"], 2)

            def gla_att(hd):
                p, b = hd // 2, 64 * (hd % 2)
                if hd >= 2:
                    pe.wait_ge(gla["masked"], hd - 1)
                for t in range(TT):
                    tk = slice(t * P, (t + 1) * P)
                    last = mm(aux[hd % 2][:, tk], ak[b:b + 64, p, tk], aq[b:b + 64, p, tk], start=True, stop=True)
                last.then_inc(gla["att"], 1)

            gla_att(0)
            pe.wait_ge(gla["state"], 28)
            for hd in range(4):
                p, b = hd // 2, 64 * (hd % 2)
                if hd < 3:
                    gla_att(hd + 1)
                pe.wait_ge(gla["masked"], hd + 1)
                if hd >= 2:
                    pe.wait_ge(gla["taken"], hd - 1)
                o = aux[2 + hd % 2]
                for t in range(TT):
                    tk = slice(t * P, (t + 1) * P)
                    last = mm(o[:, tk], av[:, t, hd * P:(hd + 1) * P], attm[:, hd % 2, tk], start=True, stop=False,
                              skip_group_check=True)
                    for n in (2 * t, 2 * t + 1):
                        if n:
                            last = mm(o[:, 64 * n:64 * n + 64], gst[b:b + 64, p, n - 1, :],
                                      aq[b:b + 64, p, 64 * n:64 * n + 64], start=False, stop=True,
                                      skip_group_check=True)
                last.then_inc(gla["out"], 1)
            head_stats("gla", [0] * 4, 128, None)
            head_stats("qk", [0] * 8, 64, None)
            pe.wait_ge(lam_sem["prod"], 1)
            mm(aux[2][:, 0:2], ones, small[:, 0:2], start=True, stop=True).then_inc(lam_sem["sum"], 1)
            pe.wait_ge(hn["out"], HN["qk"][0] + 8)

            def diff_scores(n, dst):
                hd, t = DIFF_U[n]
                for c in range(2):
                    last = mm(dst[c][:, 0:(t + 1) * P], bq[64 * c:64 * c + 64, hd, t * P:(t + 1) * P],
                              bk[64 * c:64 * c + 64, hd, 0:(t + 1) * P], start=True, stop=True)
                return last

            def diff_mix(n):
                hd, t = DIFF_U[n]
                if t == 0 and hd >= 2:
                    pe.wait_ge(sem_diff["taken"], hd - 1)
                for b in range(t + 1):
                    last = mm(aux[2 + hd % 2][:, t * P:(t + 1) * P], bv[:, b, hd * P:(hd + 1) * P],
                              dtmp[2][:, n % 2, b * P:(b + 1) * P], start=(b == 0), stop=(b == t))
                return last

            attention(sem_diff, DIFF_U, diff_scores, lambda n: DIFF_U[n][1] + 1, dtmp[1], dtmp[2], diff_mix)
            head_stats("diff", [0] * 4, 128, None)
            slabs_and_stats(slab_of("even_out"), h_hi, h_lo, DC, S, "cffn0", split0=SPLIT["even"][0])

            ffn("conv0", "cffn0", S, "mix1")

            for ps in range(2):
                s = slab_of(f"odd_in{ps}")
                if ps == 0:
                    slabs(s, 6, h_hi, h_lo, DC, S, split0=SPLIT["mix1"][0])
                else:
                    slabs(s, 6, h_hi, h_lo, DC, S)
                for g in range(3):
                    cls = [slice(t * P, (t + 1) * P) if g == 0 else slice(t, S, 4) for t in range(4)]
                    slab_tokens(s + 6 + g, (s + 6 + g) % 2, cls)
                projections_taken(pe, f"odd_in{ps}")
                head_stats(f"odd{ps}", [0] * 12, 128, None)
                pe.wait_ge(hn["out"], HN[f"odd{ps}"][0] + 12)

                def odd_scores(n, dst):
                    hh, r = ODD_U[n % 8]
                    mm(dst[0][:], oq[:, hh, r:S:4], okk[:, hh, :], start=True, stop=True)
                    for g in (1, 2):
                        last = mm(dst[1][:, (g - 1) * P:g * P], oq[:, 2 * g + hh, r:S:4], okk[:, 2 * g + hh, r:S:4],
                                  start=True, stop=True)
                    return last

                def odd_mix(n):
                    hh, r = ODD_U[n % 8]
                    if r == 0 and n // 4 >= 2:
                        pe.wait_ge(sem_odd["taken"], n // 4 - 1)
                    o = aux[2 + hh % 2][:, r * P:(r + 1) * P]
                    for b in range(6):
                        v = ov[:, 0, b, hh * P:(hh + 1) * P] if b < 4 else ov[:, b - 3, r, hh * P:(hh + 1) * P]
                        last = mm(o, v, oWT[:, n % 2, b * P:(b + 1) * P], start=(b == 0), stop=(b == 5))
                    return last

                U = 8
                n0 = 8 * ps

                def turn(n):
                    pe.wait_ge(sem_odd["weights"], n + 1)
                    if n >= 1:
                        pe.wait_ge(sem_odd["copied"], n)
                    for b in range(6):
                        last = nc.tensor.transpose(aux[b // 4][:, (b % 4) * P:(b % 4) * P + P],
                                                   oW[:, n % 2, b * P:(b + 1) * P], ident)
                    last.then_inc(sem_odd["turned"], 1)

                def score(n):
                    if n >= n0 + 2:
                        pe.wait_ge(sem_odd["probs"], n - 1)
                    odd_scores(n, acc[n % 2]).then_inc(sem_odd["scores"], 1)

                score(n0)
                score(n0 + 1)
                for n in range(n0, n0 + U):
                    turn(n)
                    if n + 2 < n0 + U:
                        score(n + 2)
                    pe.wait_ge(sem_odd["copied"], n + 1)
                    odd_mix(n).then_inc(sem_odd["mixed"], 1)
            slabs_and_stats(slab_of("odd_out"), h_hi, h_lo, 4, S, "cffn1", split0=SPLIT["odd"][0])

            ffn("conv1", "cffn1", S, "m00")
            ffn("ffn00", "m00", S, "m01")

            s = slab_of("a_in")
            slab_out(s, s % 2, h_hi, h_lo, DC, S, split0=SPLIT["m01"][0])
            slab_out(s + 1, (s + 1) % 2, h_hi, h_lo, DC, S)
            slot = (s + 2) % 2
            slab_split(s + 2)
            for kc in range(DC):
                o = acc[slot][0][:]
                mm(o, w_tile(whi, slot, kc, 0), h_hi[:, kc, :], start=(kc == 0), stop=False)
                mm(o, w_tile(whi, slot, kc, 0), h_lo[:, kc, :], start=False, stop=False)
                mm(o, w_tile(wlo, slot, kc, 0), h_hi[:, kc, :], start=False, stop=(kc == 7))
            for i in range(4):
                o = acc[slot][1][:, P * i:P * i + P]
                for kc in range(DC):
                    a_h, a_l = h_hi[:, kc, i * P:(i + 1) * P], h_lo[:, kc, i * P:(i + 1) * P]
                    mm(o, a_h, w_tile(whi, slot, kc, 1), start=(kc == 0), stop=False)
                    mm(o, a_l, w_tile(whi, slot, kc, 1), start=False, stop=False)
                    last = mm(o, a_h, w_tile(wlo, slot, kc, 1), start=False, stop=(kc == 7))
            last.then_inc(slab_done, 1)
            slab_out(s + 3, (s + 3) % 2, h_hi, h_lo, DC, S)
            slab_out(s + 4, (s + 4) % 2, h_hi, h_lo, DC, S)
            projections_taken(pe, "a_in")
            head_stats("a", [0] * 5, 64, None)
            pe.wait_ge(stage_loaded, 80)
            for i in range(5):
                pe.wait_ge(hn["out"], HN["a"][0] + i + 1)
                if i >= 2:
                    pe.wait_ge(rope["done"], i - 1)
                src = qa[:, i, :] if i < 4 else kall[:, CTX:]
                mm(aux[2 + i % 2][:], ka[:, KA_ROT:KA_ROT + P], src, start=True, stop=True).then_inc(rope["rot"], 1)
            pe.wait_ge(rope["done"], 5)

            def a_scores(n, dst):
                hd, t = A_U[n]
                b = 64 * (hd // 4)
                q = qa[b:b + 64, hd % 4, t * P:(t + 1) * P]
                mm(dst[0][:], q, kall[b:b + 64, 0:512], start=True, stop=True)
                return mm(dst[1][:, 0:256], q, kall[b:b + 64, 512:768], start=True, stop=True)

            def a_mix(n):
                hd, t = A_U[n]
                b = 64 * (hd // 4)
                if t == 0 and hd >= 2:
                    pe.wait_ge(sem_a["taken"], hd - 1)
                for k in range(6):
                    last = mm(aux[2 + hd % 2][b:b + 64, t * P:(t + 1) * P], vall[:, k, b:b + 64],
                              aWT[:, n % 2, k * P:(k + 1) * P], start=(k == 0), stop=(k == 5))
                return last

            attention(sem_a, A_U, a_scores, lambda n: 6, aW, aWT, a_mix)
            for g in range(4):
                pe.wait_ge(poolm["diff"], g + 1)
                mm(acc[g // 2][g % 2][:], wpool[:, g, :], pd[:, g, :], start=True, stop=True)\
                    .then_inc(poolm["mixed"], 1)
            pe.wait_ge(stg_ready, SPLIT["a"][0] + 8)
            slabs_and_stats(slab_of("a_out"), h_hi, h_lo, DC, S, "m02", split0=SPLIT["a"][0])

            ffn("ffn01", "m02", S, "m10")
            ffn("ffn10", "m10", S, "m11")

            s = slab_of("c_in")
            slab_out(s, s % 2, h_hi, h_lo, DC, S, split0=SPLIT["m11"][0])
            for i in range(1, 4):
                slab_out(s + i, (s + i) % 2, h_hi, h_lo, DC, S)
            for i in range(4):
                slab_tokens(s + 4 + i, (s + 4 + i) % 2, toks)
            pe.wait_ge(cmix["v"], TT)
            pe.wait_ge(stage_loaded, 112)
            for g in range(8):
                if g >= 2:
                    pe.wait_ge(cmix["sv"], g - 1)
                for t in range(TT):
                    last = mm(aux[2 + g % 2][:, t * P:(t + 1) * P], vt[:, t, g * P:(g + 1) * P], wsp[:, g, :],
                              start=True, stop=True)
                last.then_inc(cmix["mixed"], 1)
            slabs_and_stats(slab_of("c_out"), h_hi, h_lo, DC, S, "m12", split0=SPLIT["c"][0])
            ffn("ffn11", "m12", S, None)

        @block.scalar
        def _(act):
            step = [0]

            def link(ins):
                step[0] += 1
                ins.then_inc(act_step, 1)
                act.wait_ge(act_step, step[0])

            A = nc.scalar.activation

            def split_w(s, slot, at=None, first=False):
                e = s if at is None else at
                act.wait_ge(raw_loaded[slot], 16 * (s // 2 + 1) if at is None else at)
                if not first:
                    act.wait_ge(slab_done, e - 1)
                A(whi[:, slot, :], raw[:, slot, :], ACT.Copy).then_inc(whi_done, 1)

            def split_next(s):
                if s + 2 < NSLAB:
                    act.wait_ge(raw_loaded[s % 2], 16 * ((s + 2) // 2 + 1))
                    act.wait_ge(slab_done, s + 1)
                    A(whi[:, s % 2, :], raw[:, s % 2, :], ACT.Copy).then_inc(whi_done, 1)

            def split_next_in_loop(s, i):
                act.wait_ge(raw_loaded[s % 2], 16 * ((s + 2) // 2 + 1) + 16 * i)
                act.wait_ge(slab_done, s + 1 + 2 * i)
                A(whi[:, s % 2, :], raw[:, s % 2, :], ACT.Copy).then_inc(whi_done, 1)

            def square(norm, c, T):
                needs_round(act, norm, c)
                n = 8 * NORM[norm] + c
                if n >= 2:
                    act.wait_ge(stat_done, n - 1)
                A(sq[:, n % 2, 0:T], x[:, c, 0:T], ACT.Square).then_inc(sq_ready, 1)

            def inv_rms(src, tmp, dst):
                link(A(tmp, src, ACT.Ln, bias=par[:, PC["eps"]:PC["eps"] + 1]))
                return A(dst, tmp, ACT.Exp, scale=-0.5)

            def norm(name, T):
                k = NORM[name]
                act.wait_ge(stat_done, 8 * k + 8)
                if hn_count[0]:
                    act.wait_ge(hn["out"], hn_count[0])
                inv_rms(aux[0][:, 0:T], rstd[:, 1, 0:T], rstd[:, 0, 0:T]).then_inc(rstd_ready, 1)
                n0 = SPLIT[name][0]
                for c in range(8):
                    split_hi(n0 + c, h_hi[:, c, 0:T], T)

            hn_count = [0]

            def split_hi(n, dst, T=S):
                act.wait_ge(stg_ready, n + 1)
                A(dst, stg[:, n % 2, 0:T], ACT.Copy).then_inc(hi_done, 1)

            def head_norm(name, srcs, ready=None, T=S):
                n0 = HN[name][0]
                cnt = len(srcs)

                def sqr(i):
                    n = n0 + i
                    if ready:
                        ready(i)
                    if n >= 2:
                        act.wait_ge(hn["stat"], n - 1)
                    A(sq[:, n % 2, 0:T], srcs[i], ACT.Square).then_inc(hn["sq"], 1)

                sqr(0)
                for i in range(cnt):
                    n = n0 + i
                    if i + 1 < cnt:
                        sqr(i + 1)
                    act.wait_ge(hn["stat"], n + 1)
                    if n >= 1:
                        act.wait_ge(hn["out"], n)
                    inv_rms(aux[n % 2][:, 0:T], rstd[:, 1, 0:T], rstd[:, 0, 0:T]).then_inc(hn["rstd"], 1)
                hn_count[0] = n0 + cnt

            def ffn(name, kind, T, layer, norm_name):
                s0, n0 = slab_of(name), SPLIT[name][0]
                half_i = [None]

                def chunk(s, slot, c, i2, n, dst):
                    b = (n) % 2
                    g, v = acc[slot][0][:, 0:T], acc[slot][1][:, 0:T]
                    act.wait_ge(slab_done, s + 1 + i2)
                    if kind == "conv":
                        wc = PC["conv_w"] + layer * 3 * 2 * FC
                        bc = PC["conv_b"] + layer * 2 * FC
                        act.wait_ge(stg_ready, n - 1 + i2)
                        A(cg[:, b, 0:T], g, ACT.Identity, scale=par[:, bass.ds(wc + 2 * 2 * FC + c + i2, 1)],
                          bias=par[:, bass.ds(bc + c + i2, 1)]).then_inc(center_done, 1)
                        A(cv[:, b, 0:T], v, ACT.Identity, scale=par[:, bass.ds(wc + 2 * 2 * FC + FC + c + i2, 1)],
                          bias=par[:, bass.ds(bc + FC + c + i2, 1)]).then_inc(center_done, 1)
                    else:
                        act.wait_ge(stg_ready, n - 1 + i2)
                        A(sg[:, b, 0:T], g, ACT.Silu).then_inc(silu_done, 1)
                    if isinstance(i2, int):
                        split_next(s)
                    else:
                        split_next_in_loop(s, half_i[0])
                    if kind == "conv":
                        act.wait_ge(tap_done, 4 * (CONV_CH[name] + c) + 2 + 4 * i2)
                        A(sg[:, b, 0:T], cg[:, b, 0:T], ACT.Silu).then_inc(silu_done, 1)
                    act.wait_ge(stg_ready, n + 1 + i2)
                    A(dst, stg[:, b, 0:T], ACT.Copy).then_inc(hi_done, 1)

                def up(s, c0, cnt, slot_mid):
                    assert (n0 + c0) % 2 == 0
                    for j in range(2):
                        chunk(s + j, (s + j) % 2, c0 + j, 0, n0 + c0 + j, mid_hi[:, slot_mid, j, 0:T])
                    with act.Fori(0, cnt // 2 - 1) as i:
                        half_i[0] = i
                        for j in range(2):
                            chunk(s + 2 + j, (s + j) % 2, c0 + 2 + j, 2 * i, n0 + c0 + 2 + j,
                                  mid_hi[:, slot_mid, bass.ds(2 * i + 2 + j, 1), 0:T])

                up(s0, 0, 8, 0)
                up(s0 + 8, 8, 8, 1)
                for s in range(s0 + 16, s0 + 20):
                    split_next(s)
                up(s0 + 20, 16, 6, 0)
                for s in range(s0 + 26, s0 + 30):
                    split_next(s)
                last_round(s0 + 30, norm_name, T)

            def last_round(s0, norm_name, T):
                for i in range(4):
                    split_next(s0 + i)
                    if norm_name:
                        square(norm_name, 2 * i, T)
                        square(norm_name, 2 * i + 1, T)

            def attention(sems, units, n0, width, ncomp, scale, p_ap, wt_ap, nblocks, base):
                def expo(n):
                    act.wait_ge(sems["negmax"], n + 1)
                    if n >= n0 + 2:
                        act.wait_ge(sems["weights"], n - 1)
                    b = n % 2
                    for c in range(ncomp):
                        if ncomp == 2:
                            w = width(n)
                            last = A(p_ap[:, b, c * S:c * S + w], acc[b][c][:, 0:w], ACT.Exp, scale=scale,
                                     bias=small[:, base + 2 * b + c:base + 2 * b + c + 1],
                                     accum_out=small[:, base + 4 + 4 * b + c:base + 5 + 4 * b + c])
                        else:
                            for k, w in ((0, 512), (1, 256)):
                                last = A(p_ap[:, b, 512 * k:512 * k + w], acc[b][k][:, 0:w], ACT.Exp, scale=scale,
                                         bias=small[:, base + 2 * b:base + 2 * b + 1],
                                         accum_out=small[:, base + 4 + 4 * b + k:base + 5 + 4 * b + k])
                    last.then_inc(sems["probs"], 1)

                def copy(n):
                    act.wait_ge(sems["turned"], n + 1)
                    if n >= 2:
                        act.wait_ge(sems["mixed"], n - 1)
                    nb = nblocks(n)
                    last = A(wt_ap[:, n % 2, 0:min(nb, 4) * P], aux[0][:, 0:min(nb, 4) * P], ACT.Copy)
                    if nb > 4:
                        last = A(wt_ap[:, n % 2, 512:nb * P], aux[1][:, 0:(nb - 4) * P], ACT.Copy)
                    last.then_inc(sems["copied"], 1)

                expo(n0)
                for n in range(n0, n0 + len(units)):
                    if n + 1 < n0 + len(units):
                        expo(n + 1)
                    copy(n)

            def take(name, i, dst, func=ACT.Copy, w=S):
                s = slab_of(name, i)
                act.wait_ge(slab_done, s + 1)
                if dst is not None:
                    A(dst, acc[s % 2][0][0:dst.shape[0], 0:w], func)
                split_next(s)

            act.wait_ge(par_loaded, 32)
            A(csil[:], par[:, PC["c2"]:PC["c2"] + 16], ACT.Silu).then_inc(csil_ready, 1)
            for b in range(2):
                act.wait_ge(raw_loaded[b], 16)
                A(whi[:, b, :], raw[:, b, :], ACT.Copy).then_inc(whi_done, 1)
            act.wait_ge(csil_ready, 1)
            act.wait_ge(cT_ready, 1)
            for k in range(8):
                A(cT[:, k, 0:1], csil[:, k:k + 1], ACT.Copy).then_inc(cT_ready, 1)
                A(cT[:, k, 2:3], csil[:, 8 + k:9 + k], ACT.Copy).then_inc(cT_ready, 1)
            with act.Fori(0, 36) as i:
                for j in range(2):
                    split_next_in_loop(j, i)

            for c in range(8):
                square("ctx0", c, CTX)
            norm("ctx0", CTX)
            ffn("ctx_ffn", "swiglu", CTX, 0, "ctx1")
            norm("ctx1", CTX)
            take("ctx_kv", 0, kctx[:], w=CTX)
            act.wait_ge(whi_done, slab_of("ctx_kv") + 3)
            head_norm("ctx", [kctx[:]], T=CTX)

            for c in range(8):
                square("mix0", c, S)
            norm("mix0", S)
            act.wait_ge(slab_done, slab_of("ctx_kv"))
            act.dma_start(ke[:], k_even).then_inc(stage_loaded, 16)
            act.dma_start(wa2[:], w_a2).then_inc(stage_loaded, 16)
            take("even_in", 0, arT[:])
            take("even_in", 1, aq[:, 0, :])
            take("even_in", 2, ak[:, 0, :])
            for i in range(2):
                s = slab_of("even_in", 3 + i)
                act.wait_ge(slab_done, s + 1)
                for j in range(2):
                    A(sag[:, 2 * i + j, :], acc[s % 2][j][:], ACT.Silu)
                split_next(s)
            for i in range(2):
                take("even_in", 5 + i, bq[:, 2 * i, :])
            for i in range(2):
                take("even_in", 7 + i, bk[:, 2 * i, :])
            for i in range(4):
                s = slab_of("even_in", 9 + i)
                act.wait_ge(slab_done, s + 1)
                dst = (av, av, bv, bv)[i]
                A(dst[:, 0:2, 256 * (i % 2):256 * (i % 2) + 256],
                  acc[s % 2][0][:].rearrange("p (t n) -> p t n", n=256), ACT.Copy)
                split_next(s)
            projections_taken(act, "even_in")
            ba = PC["b_a"]
            for p in range(2):
                act.wait_ge(gla["la"], p + 1)
                link(A(gt[:, 0, :], aux[p][:], ACT.Abs, bias=par[:, ba + p:ba + p + 1]))
                link(A(gt[:, 1, :], gt[:, 0, :], ACT.Exp, scale=-1.0))
                A(kk[:, p, :], gt[:, 1, :], ACT.Ln, bias=ones[:, 0:1]).then_inc(gla["abs"], 1)
            act.wait_ge(gla["abs"], 2)
            for p in range(2):
                act.wait_ge(gla["b"], 2 * p + 1)
                if p:
                    act.wait_ge(gla["eb"], 2)
                A(gt[:, 0, :], gb[:, p, :], ACT.Exp, scale=1.0 / 16)
                A(gt[:, 1, :], gb[:, p, :], ACT.Exp, scale=-1.0 / 16)
                A(decay[:, p, :], gb[:, p, 63:S:64], ACT.Exp, scale=1.0 / 16)
                act.wait_ge(gla["b"], 2 * p + 2)
                A(gt[:, 3, :], gt[:, 2, :], ACT.Exp, scale=1.0 / 16).then_inc(gla["lastdiff"], 1)
            for p in range(2):
                act.wait_ge(gla["turned"], p + 1)
                A(kkT[:, p, :], aux[2 + p][:], ACT.Copy).then_inc(gla["copied"], 1)
            head_norm("gla", [gt[:, j, :] for j in range(4)], ready=lambda i: act.wait_ge(gla["taken"], i + 1))
            for j in range(4):
                split_hi(SPLIT["even"][0] + j, h_hi[:, j, :])
            head_norm("qk", [bq[:, j, :] for j in range(4)] + [bk[:, j, :] for j in range(4)])
            act.wait_ge(lam_sem["sum"], 1)
            A(small[:, 2:4], aux[2][:, 0:2], ACT.Exp).then_inc(lam_sem["exp"], 1)
            attention(sem_diff, DIFF_U, 0, lambda n: (DIFF_U[n][1] + 1) * P, 2, 0.125, dtmp[0], dtmp[2],
                      lambda n: DIFF_U[n][1] + 1, 8)
            head_norm("diff", [bq[:, j, :] for j in range(4)], ready=lambda i: act.wait_ge(sem_diff["taken"], i + 1))
            for j in range(4):
                split_hi(SPLIT["even"][0] + 4 + j, h_hi[:, 4 + j, :])
            last_round(slab_of("even_out"), "cffn0", S)
            norm("cffn0", S)
            ffn("conv0", "conv", S, 0, "mix1")

            norm("mix1", S)
            act.wait_ge(slab_done, slab_of("odd_in0"))
            act.dma_start(ko[:], k_odd).then_inc(stage_loaded, 16)
            for ps in range(2):
                nm = f"odd_in{ps}"
                if ps:
                    act.wait_ge(sem_odd["mixed"], 8)
                for g in range(3):
                    take(nm, 2 * g, oq[:, 2 * g, :])
                    take(nm, 2 * g + 1, okk[:, 2 * g, :])
                for g in range(3):
                    s = slab_of(nm, 6 + g)
                    act.wait_ge(slab_done, s + 1)
                    A(ov[:, g, 0:2, :], acc[s % 2][0][:].rearrange("p (t n) -> p t n", n=256), ACT.Copy)
                    split_next(s)
                projections_taken(act, nm)
                head_norm(f"odd{ps}", [oq[:, j, :] for j in range(6)] + [okk[:, j, :] for j in range(6)])
                attention(sem_odd, ODD_U, 8 * ps, None, 1, 128.0 ** -0.5, oP, oWT, lambda n: 6, 8)
            for j in range(4):
                split_hi(SPLIT["odd"][0] + j, h_hi[:, j, :])
            last_round(slab_of("odd_out"), "cffn1", S)
            norm("cffn1", S)
            ffn("conv1", "conv", S, 1, "m00")
            norm("m00", S)
            ffn("ffn00", "swiglu", S, 0, "m01")

            norm("m01", S)
            act.wait_ge(slab_done, slab_of("a_in"))
            act.dma_start(ka[:], k_a).then_inc(stage_loaded, 16)
            act.dma_start(wpool[:], pool_w.rearrange("g p n -> p g n")).then_inc(stage_loaded, 16)
            take("a_in", 0, qa[:, 0, :])
            take("a_in", 1, qa[:, 2, :])
            take("a_in", 2, kall[:, CTX:])
            take("a_in", 3, pp[:, 0, 8:8 + S])
            take("a_in", 4, pp[:, 2, 8:8 + S])
            projections_taken(act, "a_in")
            head_norm("a", [qa[:, j, :] for j in range(4)] + [kall[:, CTX:]])
            attention(sem_a, A_U, 0, None, 1, 0.125, aP, aWT, lambda n: 6, 8)
            for j in range(8):
                split_hi(SPLIT["a"][0] + j, h_hi[:, j, :])
            last_round(slab_of("a_out"), "m02", S)
            norm("m02", S)
            ffn("ffn01", "swiglu", S, 0, "m10")
            norm("m10", S)
            ffn("ffn10", "swiglu", S, 0, "m11")

            norm("m11", S)
            act.wait_ge(slab_done, slab_of("c_in"))
            act.dma_start(wsp[:], w_spT.rearrange("g q p -> q g p")).then_inc(stage_loaded, 16)
            act.dma_start(bsp[:], b_sp).then_inc(stage_loaded, 16)
            for i in range(4):
                s = slab_of("c_in", i)
                act.wait_ge(slab_done, s + 1)
                for j in range(2):
                    A(u[:, 2 * i + j, :], acc[s % 2][j][:], ACT.Gelu_apprx_tanh)
                split_next(s)
            for i in range(4):
                s = slab_of("c_in", 4 + i)
                act.wait_ge(slab_done, s + 1)
                for j in range(2):
                    A(vt[:, 2 * j:2 * j + 2, 256 * i:256 * i + 256],
                      acc[s % 2][j][:].rearrange("p (t n) -> p t n", n=256), ACT.Gelu_apprx_tanh)
                split_next(s)
            act.wait_ge(whi_done, slab_of("c_out") + 2)
            for t in range(TT):
                A(sv[:].rearrange("p b n -> p (b n)"), vt[:, t, :], ACT.Square, accum_out=vss[:, t:t + 1])\
                    .then_inc(cmix["ss"], 1)
                act.wait_ge(cmix["ss"], t + 1)
            link(A(vss[:, 4:8], vss[:, 0:4], ACT.Ln, scale=1.0 / D, bias=par[:, PC["eps"]:PC["eps"] + 1]))
            A(vss[:, 8:12], vss[:, 4:8], ACT.Exp, scale=-0.5).then_inc(cmix["rs"], 1)
            act.wait_ge(cmix["rs"], 1)
            for t in range(TT):
                A(vt[:, t, :], vt[:, t, :], ACT.Copy, scale=vss[:, 8 + t:9 + t]).then_inc(cmix["v"], 1)
            for j in range(8):
                split_hi(SPLIT["c"][0] + j, h_hi[:, j, :])
            last_round(slab_of("c_out"), "m12", S)
            norm("m12", S)
            ffn("ffn11", "swiglu", S, 0, None)

        @block.vector
        def _(dve):
            V = nc.vector
            step = [0]

            def link(ins):
                step[0] += 1
                ins.then_inc(dve_step, 1)
                dve.wait_ge(dve_step, step[0])

            WD = SLAB - WPOOL

            def split_next(s):
                if s + 2 < NSLAB:
                    dve.wait_ge(whi_done, s + 3)
                    dve.wait_ge(slab_done, s + 1)
                    V.tensor_tensor(wlo[:, s % 2, 0:WD], raw[:, s % 2, 0:WD], whi[:, s % 2, 0:WD].bitcast(F32),
                                    ALU.subtract).then_inc(wlo_done, 1)

            def split_next_in_loop(s, i):
                dve.wait_ge(whi_done, s + 3 + 2 * i)
                dve.wait_ge(slab_done, s + 1 + 2 * i)
                V.tensor_tensor(wlo[:, s % 2, 0:WD], raw[:, s % 2, 0:WD], whi[:, s % 2, 0:WD].bitcast(F32),
                                ALU.subtract).then_inc(wlo_done, 1)

            def stg_free(n, at=None):
                if n >= 2:
                    dve.wait_ge(hi_done, (n if at is None else at) - 1)
                    dve.wait_ge(lo_done, (n if at is None else at) - 1)

            def norm(name, T, scale_col, shift=None):
                dve.wait_ge(rstd_ready, NORM[name] + 1)
                n0 = SPLIT[name][0]
                for c in range(8):
                    n = n0 + c
                    needs_round(dve, name, c)
                    stg_free(n)
                    y = stg[:, n % 2, 0:T]
                    ins = V.scalar_tensor_tensor(out=y, in0=x[:, c, 0:T], scalar=scale_col(c), in1=rstd[:, 0, 0:T],
                                                 op0=ALU.mult, op1=ALU.mult)
                    if shift is not None:
                        link(ins)
                        k, w = shift
                        ins = V.tensor_scalar(y, y, modT[:, k + c, w:w + 1], None, ALU.add)
                    ins.then_inc(stg_ready, 1)

            def residual(s, r, T, gate):
                i = s[1]
                dve.wait_ge(slab_done, s[0] + i + 1)
                for j in range(2):
                    c = 2 * i + j
                    if r is not None and r >= 1:
                        dve.wait_ge(x_written, 8 * (r - 1) + c + 1)
                    ps = acc[(s[0] + i) % 2][j][:, 0:T]
                    if gate is None:
                        ins = V.tensor_tensor(x[:, c, 0:T], ps, x[:, c, 0:T], ALU.add)
                    else:
                        ins = V.scalar_tensor_tensor(out=x[:, c, 0:T], in0=ps, scalar=gates[:, gate, c:c + 1],
                                                     in1=x[:, c, 0:T], op0=ALU.mult, op1=ALU.add)
                    ins.then_inc(x_written, 1)
                split_next(s[0] + i)

            def ffn(name, kind, T, layer, gate):
                s0, n0 = slab_of(name), SPLIT[name][0]
                half_i = [None]

                def chunk(s, slot, c, i2, n):
                    b = n % 2
                    g, v = acc[slot][0], acc[slot][1]
                    if kind == "conv":
                        wc = PC["conv_w"] + layer * 3 * 2 * FC
                        k0 = CONV_CH[name] + c
                        for q, (buf, ps) in enumerate(((cg, g), (cv, v))):
                            dve.wait_ge(center_done, 2 * k0 + q + 1 + 2 * i2)
                            for tap, sh in ((1, 1), (0, 2)):
                                if sh == 2:
                                    dve.wait_ge(tap_done, 4 * k0 + 2 * q + 1 + 4 * i2)
                                V.scalar_tensor_tensor(
                                    out=buf[:, b, sh:T], in0=ps[:, 0:T - sh],
                                    scalar=par[:, bass.ds(wc + tap * 2 * FC + q * FC + c + i2, 1)],
                                    in1=buf[:, b, sh:T], op0=ALU.mult, op1=ALU.add).then_inc(tap_done, 1)
                        if isinstance(i2, int):
                            split_next(s)
                        else:
                            split_next_in_loop(s, half_i[0])
                        dve.wait_ge(tap_done, 4 * k0 + 4 + 4 * i2)
                        right = cv[:, b, 0:T]
                    else:
                        right = v[:, 0:T]
                    dve.wait_ge(silu_done, SILU_CH[name] + c + 1 + i2)
                    dve.wait_ge(hi_done, n - 1 + i2)
                    dve.wait_ge(lo_done, n - 1 + i2)
                    V.tensor_tensor(stg[:, b, 0:T], sg[:, b, 0:T], right, ALU.mult).then_inc(stg_ready, 1)
                    if kind != "conv":
                        if isinstance(i2, int):
                            split_next(s)
                        else:
                            split_next_in_loop(s, half_i[0])

                def up(s, c0, cnt):
                    for j in range(2):
                        chunk(s + j, (s + j) % 2, c0 + j, 0, n0 + c0 + j)
                    with dve.Fori(0, cnt // 2 - 1) as i:
                        half_i[0] = i
                        for j in range(2):
                            chunk(s + 2 + j, (s + j) % 2, c0 + 2 + j, 2 * i, n0 + c0 + 2 + j)

                def round_(s, r):
                    for i in range(4):
                        residual((s, i), r, T, gate)

                r = ROUND[name, 0]
                up(s0, 0, 8)
                up(s0 + 8, 8, 8)
                round_(s0 + 16, r)
                up(s0 + 20, 16, 6)
                round_(s0 + 26, r + 1)
                round_(s0 + 30, r + 2)

            def head_norm(name, srcs, gain, dsts=None, T=S, ready=None):
                n0 = HN[name][0]
                for i, src in enumerate(srcs):
                    dve.wait_ge(hn["rstd"], n0 + i + 1)
                    if ready:
                        ready(i)
                    V.scalar_tensor_tensor(out=dsts[i] if dsts else src, in0=src, scalar=gain(i),
                                           in1=rstd[:, 0, 0:T], op0=ALU.mult, op1=ALU.mult).then_inc(hn["out"], 1)

            def attention(sems, units, n0, ncomp, scale, p_ap, w_ap, nblocks, masks, base, after=None):
                def view(n, b):
                    return None

                def negmax(n):
                    b = n % 2
                    dve.wait_ge(sems["scores"], n + 1)
                    for dst, m in masks(n, acc[b]):
                        link(V.tensor_tensor(dst, dst, m, ALU.add))
                    w = nblocks(n) * P
                    if n >= n0 + 2:
                        dve.wait_ge(sems["probs"], n - 1)
                    if ncomp == 2:
                        for c in range(2):
                            link(V.tensor_reduce(small[:, 40 + c:41 + c], acc[b][c][:, 0:w], AX_X, ALU.max))
                        V.tensor_scalar(small[:, base + 2 * b:base + 2 * b + 2], small[:, 40:42], -scale, None,
                                        ALU.mult).then_inc(sems["negmax"], 1)
                    else:
                        for k, kw in ((0, 512), (1, 256)):
                            link(V.tensor_reduce(small[:, 40 + k:41 + k], acc[b][k][:, 0:kw], AX_X, ALU.max))
                        link(V.tensor_tensor(small[:, 42:43], small[:, 40:41], small[:, 41:42], ALU.max))
                        V.tensor_scalar(small[:, base + 2 * b:base + 2 * b + 1], small[:, 42:43], -scale, None,
                                        ALU.mult).then_inc(sems["negmax"], 1)

                def weights(n):
                    b = n % 2
                    dve.wait_ge(sems["probs"], n + 1)
                    if n >= n0 + 2:
                        dve.wait_ge(sems["turned"], n - 1)
                    w = nblocks(n) * P
                    sums = small[:, base + 4 + 4 * b:base + 6 + 4 * b]
                    if ncomp == 2:
                        link(V.reciprocal(small[:, 44:46], sums))
                        link(V.tensor_tensor(small[:, 46:47], small[:, 45:46], small[:, 5:6], ALU.mult))
                        link(V.tensor_scalar(w_ap[:, b, 0:w], p_ap[:, b, 0:w], small[:, 44:45], None, ALU.mult))
                        V.scalar_tensor_tensor(out=w_ap[:, b, 0:w], in0=p_ap[:, b, S:S + w], scalar=small[:, 46:47],
                                               in1=w_ap[:, b, 0:w], op0=ALU.mult, op1=ALU.add)\
                            .then_inc(sems["weights"], 1)
                    else:
                        link(V.tensor_tensor(small[:, 44:45], sums[:, 0:1], sums[:, 1:2], ALU.add))
                        link(V.reciprocal(small[:, 45:46], small[:, 44:45]))
                        V.tensor_scalar(w_ap[:, b, 0:w], p_ap[:, b, 0:w], small[:, 45:46], None, ALU.mult)\
                            .then_inc(sems["weights"], 1)

                end = n0 + len(units)
                negmax(n0)
                for n in range(n0, end):
                    if n + 1 < end:
                        negmax(n + 1)
                    weights(n)
                    if after and n >= n0 + 1:
                        after(n - 1)
                if after:
                    after(end - 1)

            def take(name, i, dst, w=S):
                s = slab_of(name, i)
                dve.wait_ge(slab_done, s + 1)
                if dst is not None:
                    V.tensor_copy(dst, acc[s % 2][1][:, 0:w])
                split_next(s)

            for b in range(2):
                dve.wait_ge(whi_done, b + 1)
                V.tensor_tensor(wlo[:, b, 0:WD], raw[:, b, 0:WD], whi[:, b, 0:WD].bitcast(F32), ALU.subtract)\
                    .then_inc(wlo_done, 1)
            dve.wait_ge(par_loaded, 32)
            dve.wait_ge(cT_ready, 17)
            bm = PC["b_mod"]
            for k in range(8):
                for w in range(2):
                    V.tensor_tensor(cT[:, k, 2 * w + 1:2 * w + 2], csil[:, 8 * w + k:8 * w + k + 1],
                                    cT[:, k, 2 * w:2 * w + 1].bitcast(F32), ALU.subtract).then_inc(cT_lo, 1)

            def mod_take(s, slot, at, first):
                dve.wait_ge(slab_done, at + 1)
                if not first:
                    dve.wait_ge(modcol_ready, at - 1)
                V.tensor_copy(modrow[:, slot, :], acc[slot][0][0:4, 0:256]).then_inc(modrow_ready, 1)

            def mod_col(slot, at, c):
                dve.wait_ge(modcol_ready, at + 1)
                V.tensor_tensor(modT[:, bass.ds(c, 2), :], aux[slot][:, 0:4].rearrange("p (a b) -> p a b", b=2),
                                par[:, bass.ds(bm + c, 2)].unsqueeze(2).to_broadcast([P, 2, 2]), ALU.add)\
                    .then_inc(mod_done, 1)

            mod_take(0, 0, 0, True)
            split_next(0)
            mod_take(1, 1, 1, True)
            split_next(1)
            mod_col(0, 0, 0)
            with dve.Fori(0, 35) as i:
                mod_take(2, 0, 2 + 2 * i, False)
                split_next_in_loop(2, i)
                mod_col(1, 1 + 2 * i, 2 + 4 * i)
                mod_take(3, 1, 3 + 2 * i, False)
                split_next_in_loop(3, i)
                mod_col(0, 2 + 2 * i, 4 + 4 * i)
            mod_col(1, 71, 142)
            dve.wait_ge(mod_done, 72)
            ng = PC["norm_g"]
            for n, (ly, j, w) in enumerate([(0, 0, 1), (0, 1, 1)] + [(ly, j, 0) for ly in range(2) for j in range(3)]):
                sc = modT[:, 72 * ly + 8 * (3 * j + 1):72 * ly + 8 * (3 * j + 1) + 8, w]
                g = par[:, ng + 24 * ly + 8 * j:ng + 24 * ly + 8 * j + 8]
                V.scalar_tensor_tensor(out=modA[:, n, :], in0=sc, scalar=1.0, in1=g, op0=ALU.add, op1=ALU.mult)\
                    .then_inc(small_ready, 1)
            for n, (ly, j, w) in enumerate([(0, 0, 1)] + [(ly, j, 0) for ly in range(2) for j in range(3)]):
                gt_ = modT[:, 72 * ly + 8 * (3 * j + 2):72 * ly + 8 * (3 * j + 2) + 8, w]
                V.tensor_scalar(gates[:, n, :], gt_, 1.0 if j == 1 else 0.5, None, ALU.mult).then_inc(small_ready, 1)
            l4 = PC["lam4"]
            V.tensor_tensor(small[:, 0:2], par[:, l4:l4 + 2], par[:, l4 + 2:l4 + 4], ALU.mult)\
                .then_inc(lam_sem["prod"], 1)
            V.tensor_scalar(small[:, 6:7], par[:, PC["diff_gain"]:PC["diff_gain"] + 1], 0.8, None, ALU.mult)\
                .then_inc(small_ready, 1)
            dve.wait_ge(small_ready, 16)

            norm("ctx0", CTX, lambda c: modA[:, 0, c:c + 1], (0, 1))
            ffn("ctx_ffn", "swiglu", CTX, 0, 0)
            norm("ctx1", CTX, lambda c: modA[:, 1, c:c + 1], (24, 1))
            take("ctx_kv", 0, vctx[:].rearrange("p t n -> p (t n)"), w=CTX)
            dve.wait_ge(wlo_done, slab_of("ctx_kv") + 3)
            qn = PC["qkn"]
            head_norm("ctx", [kctx[:]], lambda i: par[:, qn + 1:qn + 2], T=CTX)

            norm("mix0", S, lambda c: par[:, PC["norm_mix"] + c:PC["norm_mix"] + c + 1])
            take("even_in", 0, None)
            take("even_in", 1, aq[:, 1, :])
            take("even_in", 2, ak[:, 1, :])
            for i in range(2):
                take("even_in", 3 + i, None)
            for i in range(2):
                take("even_in", 5 + i, bq[:, 2 * i + 1, :])
            for i in range(2):
                take("even_in", 7 + i, bk[:, 2 * i + 1, :])
            for i in range(4):
                s = slab_of("even_in", 9 + i)
                dve.wait_ge(slab_done, s + 1)
                dst = (av, av, bv, bv)[i]
                V.tensor_copy(dst[:, 2:4, 256 * (i % 2):256 * (i % 2) + 256],
                              acc[s % 2][1][:].rearrange("p (t n) -> p t n", n=256))
                split_next(s)
            projections_taken(dve, "even_in")
            dve.wait_ge(stage_loaded, 32)
            ba = PC["b_a"]
            for p in range(2):
                dve.wait_ge(gla["la"], p + 1)
                if p:
                    dve.wait_ge(gla["lastdiff"], 1)
                dve.wait_ge(gla["abs"], p + 1)
                link(V.tensor_scalar(gt[:, 2, :], aux[p][:], par[:, ba + p:ba + p + 1], 0.0, ALU.add, ALU.min))
                link(V.tensor_tensor(kk[:, p, :], gt[:, 2, :], kk[:, p, :], ALU.subtract))
                V.tensor_tensor_scan(gb[:, p, :], ke[:, KE_SCAN:KE_SCAN + S], kk[:, p, :], 0.0, ALU.mult, ALU.add)\
                    .then_inc(gla["b"], 1)
                dve.wait_ge(gla["b"], 2 * p + 1)
                g3 = gb[:, p, :].rearrange("p (n c) -> p n c", c=64)
                V.tensor_tensor(gt[:, 2, :].rearrange("p (n c) -> p n c", c=64),
                                g3[:, :, 63:64].to_broadcast([P, 8, 64]), g3, ALU.subtract).then_inc(gla["b"], 1)
                dve.wait_ge(gla["lastdiff"], p + 1)
                V.tensor_tensor(kk[:, p, :], ak[:, p, :], gt[:, 3, :], ALU.mult).then_inc(gla["kk"], 1)
                V.scalar_tensor_tensor(out=aq[:, p, :], in0=aq[:, p, :], scalar=0.125, in1=gt[:, 0, :],
                                       op0=ALU.mult, op1=ALU.mult).then_inc(gla["eb"], 1)
                V.tensor_tensor(ak[:, p, :], ak[:, p, :], gt[:, 1, :], ALU.mult).then_inc(gla["eb"], 1)
            link(V.memset(attm[:], 0.0))
            for n in range(7):
                dve.wait_ge(gla["kv"], n + 1)
                if n:
                    dve.wait_ge(gla["state"], 4 * n)
                for hd in range(4):
                    p, b = hd // 2, 64 * (hd % 2)
                    kv = bank[n % 4][b:b + 64, 256 * p + 128 * (hd % 2):256 * p + 128 * (hd % 2) + 128]
                    if n == 0:
                        ins = V.tensor_copy(gst[b:b + 64, p, 0, :], kv)
                    else:
                        ins = V.scalar_tensor_tensor(out=gst[b:b + 64, p, n, :], in0=gst[b:b + 64, p, n - 1, :],
                                                     scalar=decay[b:b + 64, p, n:n + 1], in1=kv, op0=ALU.mult,
                                                     op1=ALU.add)
                    ins.then_inc(gla["state"], 1)
            mask = ke[:, KE_GLA:KE_GLA + P].bitcast(U32)
            for hd in range(4):
                dve.wait_ge(gla["att"], hd + 1)
                if hd >= 2:
                    dve.wait_ge(gla["out"], hd - 1)
                for t in range(TT):
                    last = V.copy_predicated(attm[:, hd % 2, t * P:(t + 1) * P], mask,
                                             aux[hd % 2][:, t * P:(t + 1) * P])
                last.then_inc(gla["masked"], 1)
                if hd >= 1:
                    dve.wait_ge(gla["out"], hd)
                    V.tensor_copy(gt[:, hd - 1, :], aux[2 + (hd - 1) % 2][:]).then_inc(gla["taken"], 1)
            dve.wait_ge(gla["out"], 4)
            V.tensor_copy(gt[:, 3, :], aux[3][:]).then_inc(gla["taken"], 1)
            dve.wait_ge(gla["taken"], 4)
            gg = PC["gla_gain"]
            head_norm("gla", [gt[:, j, :] for j in range(4)], lambda i: par[:, gg:gg + 1])
            n0 = SPLIT["even"][0]
            dve.wait_ge(hn["out"], HN["gla"][0] + 4)
            for j in range(4):
                stg_free(n0 + j)
                V.tensor_tensor(stg[:, (n0 + j) % 2, :], gt[:, j, :], sag[:, j, :], ALU.mult).then_inc(stg_ready, 1)
            dq, dk = PC["dq_gain"], PC["dk_gain"]
            head_norm("qk", [bq[:, j, :] for j in range(4)] + [bk[:, j, :] for j in range(4)],
                      lambda i: par[:, dq:dq + 1] if i < 4 else par[:, dk:dk + 1])
            dve.wait_ge(lam_sem["exp"], 1)
            link(V.tensor_tensor(small[:, 4:5], small[:, 3:4], small[:, 2:3], ALU.subtract))
            link(V.tensor_scalar(small[:, 5:6], small[:, 4:5], LAMBDA_INIT, None, ALU.subtract))

            def diff_masks(n, dst):
                t = DIFF_U[n][1]
                return [(dst[c][:, t * P:(t + 1) * P], causal) for c in range(2)]

            def diff_after(n):
                hd, t = DIFF_U[n]
                if t == TT - 1:
                    dve.wait_ge(sem_diff["mixed"], n + 1)
                    V.tensor_copy(bq[:, hd, :], aux[2 + hd % 2][:]).then_inc(sem_diff["taken"], 1)

            attention(sem_diff, DIFF_U, 0, 2, 0.125, dtmp[0], dtmp[1], lambda n: DIFF_U[n][1] + 1, diff_masks, 8,
                      diff_after)
            dve.wait_ge(sem_diff["taken"], 4)

            def free(i):
                stg_free(n0 + 4 + i)

            head_norm("diff", [bq[:, j, :] for j in range(4)], lambda i: small[:, 6:7])
            dve.wait_ge(hn["out"], HN["diff"][0] + 4)
            for j in range(4):
                free(j)
                V.tensor_copy(stg[:, (n0 + 4 + j) % 2, :], bq[:, j, :]).then_inc(stg_ready, 1)
            for i in range(4):
                residual((slab_of("even_out"), i), None, S, None)

            nf = PC["norm_ffn"]
            norm("cffn0", S, lambda c: par[:, nf + c:nf + c + 1])
            ffn("conv0", "conv", S, 0, None)

            nmx = PC["norm_mix"]
            norm("mix1", S, lambda c: par[:, nmx + 8 + c:nmx + 9 + c])
            for ps in range(2):
                nm = f"odd_in{ps}"
                if ps:
                    dve.wait_ge(sem_odd["mixed"], 8)
                for g in range(3):
                    take(nm, 2 * g, oq[:, 2 * g + 1, :])
                    take(nm, 2 * g + 1, okk[:, 2 * g + 1, :])
                for g in range(3):
                    s = slab_of(nm, 6 + g)
                    dve.wait_ge(slab_done, s + 1)
                    V.tensor_copy(ov[:, g, 2:4, :], acc[s % 2][1][:].rearrange("p (t n) -> p t n", n=256))
                    split_next(s)
                projections_taken(dve, nm)
                gq, gk = PC["odq"], PC["odk"]
                head_norm(f"odd{ps}", [oq[:, j, :] for j in range(6)] + [okk[:, j, :] for j in range(6)],
                          lambda i: par[:, gq:gq + 1] if i < 6 else par[:, gk:gk + 1])
                dve.wait_ge(stage_loaded, 48)

                def odd_masks(n, dst):
                    r = ODD_U[n % 8][1]
                    return [(dst[0][:], ko[:, KO_NEAR + r * S:KO_NEAR + (r + 1) * S]),
                            (dst[1][:, 0:256], ko[:, KO_G1:KO_G1 + 256])]

                def odd_after(n):
                    hh, r = ODD_U[n % 8]
                    if r == 3:
                        dve.wait_ge(sem_odd["mixed"], n + 1)
                        V.tensor_copy(oo[:, n // 4, :].rearrange("p (n r) -> p r n", r=4),
                                      aux[2 + hh][:].rearrange("p (r n) -> p r n", r=4)).then_inc(sem_odd["taken"], 1)

                attention(sem_odd, ODD_U, 8 * ps, 1, 128.0 ** -0.5, oP, oW, lambda n: 6, odd_masks, 8, odd_after)
            dve.wait_ge(sem_odd["taken"], 4)
            n0 = SPLIT["odd"][0]
            for j in range(4):
                stg_free(n0 + j)
                V.tensor_copy(stg[:, (n0 + j) % 2, :], oo[:, j, :]).then_inc(stg_ready, 1)
            for i in range(4):
                residual((slab_of("odd_out"), i), ROUND["odd", 0], S, None)
            norm("cffn1", S, lambda c: par[:, nf + 8 + c:nf + 9 + c])
            ffn("conv1", "conv", S, 1, None)
            norm("m00", S, lambda c: modA[:, 2, c:c + 1], (0, 0))
            ffn("ffn00", "swiglu", S, 0, 1)

            norm("m01", S, lambda c: modA[:, 3, c:c + 1], (24, 0))
            dve.wait_ge(slab_done, slab_of("a_in"))
            V.memset(pp[:, :, 0:8], 0.0)
            V.memset(pp[:, :, 8 + S:16 + S], 0.0)
            V.tensor_copy(kall[:, 0:CTX], kctx[:])
            V.tensor_copy(vall[:, 0:2, :], vctx[:])
            take("a_in", 0, qa[:, 1, :])
            take("a_in", 1, qa[:, 3, :])
            take("a_in", 2, vall[:, 2:6, :].rearrange("p t n -> p (t n)"))
            take("a_in", 3, pp[:, 1, 8:8 + S])
            take("a_in", 4, pp[:, 3, 8:8 + S])
            projections_taken(dve, "a_in")
            head_norm("a", [qa[:, j, :] for j in range(4)] + [kall[:, CTX:]],
                      lambda i: par[:, qn:qn + 1] if i < 4 else par[:, qn + 1:qn + 2])
            dve.wait_ge(stage_loaded, 80)
            dve.wait_ge(hn["out"], HN["a"][0] + 5)
            for i in range(5):
                t_ = qa[:, i, :] if i < 4 else kall[:, CTX:]
                dve.wait_ge(rope["rot"], i + 1)
                if i:
                    dve.wait_ge(rope["done"], i)
                link(V.tensor_tensor(rot[:, 0, :], aux[2 + i % 2][:], ka[:, KA_SIN:KA_SIN + S], ALU.mult))
                link(V.tensor_tensor(rot[:, 1, :], t_, ka[:, KA_COS:KA_COS + S], ALU.mult))
                V.tensor_tensor(t_, rot[:, 0, :], rot[:, 1, :], ALU.add).then_inc(rope["done"], 1)

            def a_after(n):
                hd, t = A_U[n]
                if t == TT - 1:
                    b = 64 * (hd // 4)
                    dve.wait_ge(sem_a["mixed"], n + 1)
                    V.tensor_copy(qa[b:b + 64, hd % 4, :], aux[2 + hd % 2][b:b + 64, :]).then_inc(sem_a["taken"], 1)

            attention(sem_a, A_U, 0, 1, 0.125, aP, aW, lambda n: 6, lambda n, d: [], 8, a_after)
            dve.wait_ge(sem_a["taken"], 8)
            n0 = SPLIT["a"][0]
            for j in range(4):
                stg_free(n0 + j)
                V.tensor_copy(stg[:, (n0 + j) % 2, :], qa[:, j, :]).then_inc(stg_ready, 1)
            for g in range(4):
                dve.wait_ge(poolm["mixed"], g + 1)
                stg_free(n0 + 4 + g)
                pc = PC["pool_scale"] + g
                V.tensor_scalar(stg[:, (n0 + 4 + g) % 2, :], acc[g // 2][g % 2][:], par[:, pc:pc + 1], None,
                                ALU.mult).then_inc(stg_ready, 1)
            for i in range(4):
                residual((slab_of("a_out"), i), ROUND["a", 0], S, 2)
            norm("m02", S, lambda c: modA[:, 4, c:c + 1], (48, 0))
            ffn("ffn01", "swiglu", S, 0, 3)
            norm("m10", S, lambda c: modA[:, 5, c:c + 1], (72, 0))
            ffn("ffn10", "swiglu", S, 0, 4)

            norm("m11", S, lambda c: modA[:, 6, c:c + 1], (96, 0))
            for i in range(8):
                s = slab_of("c_in", i)
                dve.wait_ge(whi_done, s + 3)
                split_next(s)
            dve.wait_ge(stage_loaded, 112)
            vn = PC["v_norm"]
            n0 = SPLIT["c"][0]
            for g in range(8):
                dve.wait_ge(cmix["mixed"], g + 1)
                src = aux[2 + g % 2][:].rearrange("p (t n) -> p t n", n=P)
                V.scalar_tensor_tensor(out=sv[:, g % 2, :].rearrange("p (t n) -> p t n", n=P), in0=src,
                                       scalar=par[:, vn + g:vn + g + 1],
                                       in1=bsp[:, g:g + 1, :].to_broadcast([P, TT, P]), op0=ALU.mult, op1=ALU.add)\
                    .then_inc(cmix["sv"], 1)
                dve.wait_ge(cmix["sv"], g + 1)
                stg_free(n0 + g)
                V.tensor_tensor(stg[:, (n0 + g) % 2, :], sv[:, g % 2, :], u[:, g, :], ALU.mult).then_inc(stg_ready, 1)
            for i in range(4):
                residual((slab_of("c_out"), i), ROUND["c", 0], S, 5)
            norm("m12", S, lambda c: modA[:, 7, c:c + 1], (120, 0))
            ffn("ffn11", "swiglu", S, 0, 6)

        @block.gpsimd
        def _(pool):
            G = nc.gpsimd
            WD = SLAB - WPOOL
            step = [0]

            def link(ins):
                step[0] += 1
                ins.then_inc(pool_step, 1)
                pool.wait_ge(pool_step, step[0])

            def split_w(slot, whi_at, done_at):
                pool.wait_ge(whi_done, whi_at)
                if done_at is not None:
                    pool.wait_ge(slab_done, done_at)
                G.tensor_tensor(wlo[:, slot, WD:], raw[:, slot, WD:], whi[:, slot, WD:].bitcast(F32), ALU.subtract)\
                    .then_inc(wlo_pool_done, 1)

            def splits(s0, n):
                loop = max(0, min(n, NSLAB - 2 - s0)) // 2
                if loop > 1:
                    with pool.Fori(0, loop) as i:
                        for j in range(2):
                            split_w((s0 + j) % 2, s0 + j + 3 + 2 * i, s0 + j + 1 + 2 * i)
                else:
                    loop = 0
                for s in range(s0 + 2 * loop, s0 + n):
                    if s + 2 < NSLAB:
                        split_w(s % 2, s + 3, s + 1)

            def split_h(name, T=S, first=0, count=8):
                for c in range(first, first + count):
                    n = SPLIT[name][0] + c
                    pool.wait_ge(hi_done, n + 1)
                    G.tensor_tensor(h_lo[:, c, 0:T], stg[:, n % 2, 0:T], h_hi[:, c, 0:T].bitcast(F32), ALU.subtract)\
                        .then_inc(lo_done, 1)

            def ffn(name, T):
                s0, n0 = slab_of(name), SPLIT[name][0]

                def up(s, c0, cnt, slot_mid):
                    with pool.Fori(0, cnt // 2) as i:
                        for j in range(2):
                            split_w((s + j) % 2, s + j + 3 + 2 * i, s + j + 1 + 2 * i)
                            pool.wait_ge(hi_done, n0 + c0 + j + 1 + 2 * i)
                            G.tensor_tensor(mid_lo[:, slot_mid, bass.ds(2 * i + j, 1), 0:T],
                                            stg[:, (n0 + c0 + j) % 2, 0:T].unsqueeze(1),
                                            mid_hi[:, slot_mid, bass.ds(2 * i + j, 1), 0:T].bitcast(F32),
                                            ALU.subtract).then_inc(lo_done, 1)

                up(s0, 0, 8, 0)
                up(s0 + 8, 8, 8, 1)
                splits(s0 + 16, 4)
                up(s0 + 20, 16, 6, 0)
                splits(s0 + 26, 8)

            G.memset(cT[:].bitcast(F32), 0.0).then_inc(cT_ready, 1)
            for b in range(2):
                split_w(b, b + 1, None)
            splits(0, 72)
            split_h("ctx0", CTX)
            ffn("ctx_ffn", CTX)
            split_h("ctx1", CTX)
            splits(slab_of("ctx_kv"), 1)
            split_h("mix0")
            splits(slab_of("even_in"), 13)
            split_h("even", count=4)
            split_h("even", first=4, count=4)
            splits(slab_of("even_out"), 4)
            split_h("cffn0")
            ffn("conv0", S)
            split_h("mix1")
            splits(slab_of("odd_in0"), 18)
            split_h("odd", count=4)
            splits(slab_of("odd_out"), 4)
            split_h("cffn1")
            ffn("conv1", S)
            split_h("m00", S)
            ffn("ffn00", S)
            split_h("m01", S)
            splits(slab_of("a_in"), 5)
            projections_taken(pool, "a_in")
            pool.wait_ge(stage_loaded, 80)
            W = 16 + S
            for g, win in enumerate(POOL_WINDOWS):
                src, k, bufs = pp[:, g, :], 1, [pa, pb]
                while k < win:
                    dst = bufs[0][:]
                    link(G.tensor_copy(dst[:, 0:k], src[:, 0:k]))
                    link(G.tensor_tensor(dst[:, k:W], src[:, k:W], src[:, 0:W - k], ALU.add))
                    src, k, bufs = dst, 2 * k, bufs[::-1]
                off = 8 + win // 2 - 1
                link(G.tensor_tensor(pd[:, g, :], src[:, off:off + S], ka[:, KA_CNT + g * S:KA_CNT + (g + 1) * S],
                                     ALU.mult))
                G.tensor_tensor(pd[:, g, :], pd[:, g, :], pp[:, g, 8:8 + S], ALU.subtract).then_inc(poolm["diff"], 1)

            split_h("a")
            splits(slab_of("a_out"), 4)
            split_h("m02", S)
            ffn("ffn01", S)
            split_h("m10", S)
            ffn("ffn10", S)
            split_h("m11", S)
            splits(slab_of("c_in"), 8)
            split_h("c")
            splits(slab_of("c_out"), 4)
            split_h("m12", S)
            ffn("ffn11", S)


def columns(a):
    a = np.asarray(a, np.float32).reshape(-1)
    if a.size < P:
        a = np.concatenate([a, np.zeros(P - a.size, np.float32)])
    return a.reshape(-1, P).T


def slab(w, cols):
    part = np.concatenate([w[:, a:b] for a, b in cols], axis=1)
    out = np.zeros((8 * P, 256), np.float32)
    out[:part.shape[0], :part.shape[1]] = part
    return out.reshape(8, P, 256).transpose(1, 0, 2).reshape(P, SLAB)


def ffn_slabs(up, down):
    def ups(a, b):
        return [slab(up, [(c * P, c * P + P), (FF + c * P, FF + c * P + P)]) for c in range(a, b)]

    def downs(a, b):
        return [slab(down[a * P:b * P], [(256 * i, 256 * i + 256)]) for i in range(4)]

    (a0, b0), (a1, b1), (a2, b2) = GROUPS
    return ups(a0, b0) + ups(a1, b1) + downs(a0, b0) + ups(a2, b2) + downs(a1, b1) + downs(a2, b2)


def wide(w, at, n):
    return [slab(w, [(at + 256 * i, at + 256 * i + 256)]) for i in range(n)]


def weight_stream(i):
    g = {k: np.asarray(v) for k, v in i.items()}
    mod, w13, w2 = g["w_mod_2"], g["ffn_w13_2"], g["ffn_w2_2"]
    ev, od, wa = g["ev_w_in"][0], g["od_w_in"][0], g["w_in_a_2"][0]
    s = wide(mod[0], 0, 36) + wide(mod[1], 0, 36)
    s += ffn_slabs(w13[0, 0], w2[0, 0])
    s += wide(wa, 512, 1)
    s += [slab(ev, [(1536, 1552)])]
    s += wide(ev, 0, 2) + wide(ev, 1024, 2) + wide(ev, 1552, 2) + wide(ev, 2064, 2)
    s += wide(ev, 512, 2) + wide(ev, 2576, 2)
    s += wide(g["ev_w_out"][0], 0, 4)
    s += ffn_slabs(g["ffn_w_up"][0], g["ffn_w_down"][0])
    for ps in range(2):
        for grp in range(3):
            for q in range(2):
                s += wide(od, (grp * 3 + q) * 512 + 256 * ps, 1)
        for grp in range(3):
            s += wide(od, (grp * 3 + 2) * 512 + 256 * ps, 1)
    s += wide(g["od_w_out"][0], 0, 4)
    s += ffn_slabs(g["ffn_w_up"][1], g["ffn_w_down"][1])
    s += ffn_slabs(w13[0, 0], w2[0, 0])
    pair = [(64 * h, 64 * h + 64) for j in range(4) for h in (j, j + 4)]
    s += [slab(wa, pair[0:4]), slab(wa, pair[4:8])] + wide(wa, 512, 1) + wide(wa, 768, 2)
    woa = g["w_out_a_2"][0]
    s += wide(np.concatenate([woa[a:b] for a, b in pair] + [woa[512:]]), 0, 4)
    s += ffn_slabs(w13[0, 1], w2[0, 1])
    s += ffn_slabs(w13[1, 0], w2[1, 0])
    s += wide(g["w_in_c_2"][0], 0, 8) + wide(g["w_out_c_2"][0], 0, 4)
    s += ffn_slabs(w13[1, 1], w2[1, 1])
    assert len(s) == NSLAB
    return np.stack(s)


def parameter_table(i):
    g = {k: np.asarray(v) for k, v in i.items()}

    def both(a):
        return np.concatenate([a.reshape(-1), a.reshape(-1)])

    parts = {
        "eps": np.full(P, EPS, np.float32), "norm_mix": g["norm_mix"], "norm_ffn": g["norm_ffn"],
        "conv_w": g["ffn_conv_w"], "conv_b": g["ffn_conv_b"], "norm_g": g["norm_g_2"], "b_mod": g["b_mod_2"],
        "b_a": g["ev_b_a"], "gla_gain": g["ev_gla_gain"], "dq_gain": both(g["ev_dq_gain"]),
        "dk_gain": both(g["ev_dk_gain"]), "diff_gain": g["ev_diff_gain"],
        "odq": g["od_q_gain"], "odk": g["od_k_gain"],
        "qkn": np.concatenate([both(g["qk_norm_g_2"][0, 0]), both(g["qk_norm_g_2"][0, 1])]),
        "pool_scale": g["pool_scale_2"], "v_norm": g["v_norm_g_2"],
        "c2": np.concatenate([g["c_2"].reshape(-1), g["c_ctx_2"].reshape(-1)]),
    }
    table = np.zeros((P, NPAR), np.float32)
    for name, a in parts.items():
        c = columns(a)
        table[:, PC[name]:PC[name] + c.shape[1]] = c
    for j, name in enumerate(["ev_lq1", "ev_lq2", "ev_lk1", "ev_lk2"]):
        table[:64, PC["lam4"] + j] = g[name].reshape(-1)
    return table


def constants():
    p = np.arange(P)
    keep = np.zeros((P, NKEEP), np.float32)
    keep[:, KC_IDENT:KC_IDENT + P] = np.eye(P)
    keep[:, KC_M1024:KC_M1024 + P] = 1.0 / D
    keep[:, KC_M128:KC_M128 + P] = 1.0 / 128
    keep[:, KC_M64:KC_M64 + P] = (p[:, None] // 64 == p[None] // 64) / 64.0
    keep[:, KC_CAUSAL:KC_CAUSAL + P] = np.where(p[None] <= p[:, None], 0.0, NEG)
    keep[:, KC_ONES:KC_ONES + P] = 1.0
    keep[0:4, KC_COMB:KC_COMB + 2] = [[1, 0], [1, 0], [0, 1], [0, 1]]
    t = np.arange(S)
    even = np.zeros((P, NEVEN), np.float32)
    even[:, KE_GLA:KE_GLA + P] = (p[:, None] <= p[None]) & (p[:, None] // 64 == p[None] // 64)
    even[:, KE_SCAN:KE_SCAN + S] = t[None] % 64 != 0
    odd = np.zeros((P, NODD), np.float32)
    for r in range(4):
        dist = (r + 4 * p)[:, None] - t[None]
        odd[:, KO_NEAR + r * S:KO_NEAR + (r + 1) * S] = np.where((dist >= 0) & (dist <= 128), 0.0, NEG)
    n = p[:, None] - p[None]
    odd[:, KO_G1:KO_G1 + P] = np.where(n >= 0, 0.0, NEG)
    odd[:, KO_G2:KO_G2 + P] = np.where((n >= 0) & (n % 4 == 0), 0.0, NEG)
    a = np.zeros((P, NA), np.float32)
    inv = np.float32(10000.0) ** (-np.arange(0, 32, 2, dtype=np.float32) / np.float32(32))
    rows, cols = (t // 64).astype(np.float32), (t % 64).astype(np.float32)
    for f in range(P):
        d = f % 64
        angle = (rows if d < 32 else cols) * inv[d % 16]
        a[f, KA_COS:KA_COS + S] = np.cos(angle)
        a[f, KA_SIN:KA_SIN + S] = np.sin(angle)
        if d % 32 < 16:
            a[f + 16, KA_ROT + f] = -1.0
        else:
            a[f - 16, KA_ROT + f] = 1.0
    for g, w in enumerate(POOL_WINDOWS):
        count = np.clip(t + w // 2, 0, S) - np.clip(t - w // 2, 0, S)
        a[:, KA_CNT + g * S:KA_CNT + (g + 1) * S] = 1.0 / count
    return keep, even, odd, a


def kernel(**inputs):
    import concourse.bacc as bacc
    from concourse.bass_utils import run_bass_kernel_spmd

    g = {k: np.asarray(v) for k, v in inputs.items()}
    keep, even, odd, rotary = constants()
    arrays = {
        "stream": weight_stream(g),
        "params": parameter_table(g),
        "xT": np.ascontiguousarray(g["x"][0].T),
        "ctxT": np.ascontiguousarray(g["ctx_2"][0].T),
        "keep": keep, "k_even": even, "k_odd": odd, "k_a": rotary,
        "w_a2": np.ascontiguousarray(g["ev_w_a2"][0]),
        "pool_w": np.ascontiguousarray(g["pool_w_2"][0]),
        "w_spT": np.ascontiguousarray(g["w_sp_2"][0].transpose(0, 2, 1)),
        "b_sp": np.ascontiguousarray(np.broadcast_to(g["b_sp_2"][0][None], (P, 8, P))),
    }
    nc = bacc.Bacc("TRN2", target_bir_lowering=False, num_devices=1)
    aps = {n: nc.dram_tensor(n, a.shape, mybir.dt.from_np(a.dtype), kind="ExternalInput").ap()
           for n, a in arrays.items()}
    out = nc.dram_tensor("out", (D, S), F32, kind="ExternalOutput").ap()
    build(nc, out=out, **aps)
    r = run_bass_kernel_spmd(nc, [arrays], core_ids=[0])
    return np.ascontiguousarray(r.results[0]["out"].T)[None]
```
